# Optimizing a Trainium2 kernel written in Bass

```python
import math
import jax, jax.numpy as jnp
from jax import lax
import numpy as np

D_MODEL = 1024
BATCH = 1
SEQ = 1024
DEPTH = 1

CHUNK = 64
Q_BLOCK = 128
SPARSE_Q_BLOCK = 64
D_MIX = D_MODEL

A_HEADS = 4
A_QK_DIM = 64
A_V_DIM = 2 * A_QK_DIM
A_WIDTH = A_HEADS * A_V_DIM
A_QK_WIDTH = A_HEADS * 2 * A_QK_DIM

B_HEADS = 8
B_HEAD_DIM = 64
B_WIDTH = B_HEADS * B_HEAD_DIM
IDX_HEADS = 4
IDX_DIM = 64
TOPK_MAX = 256

N_BUCKETS = 32
MAX_DISTANCE = 128
N_BIAS_HEADS = A_HEADS + B_HEADS

EPS = 1e-6

SPLIT_SIZES = (A_QK_WIDTH, A_QK_WIDTH, A_WIDTH, A_WIDTH,
               B_WIDTH, B_WIDTH, B_WIDTH, B_WIDTH,
               IDX_HEADS * IDX_DIM, IDX_DIM, IDX_HEADS)
D_IN_PROJ = sum(SPLIT_SIZES)

kernel_name = "hybrid_diffattn_dsa_streaming_block"

def rmsnorm(x, w):
    xf = x.astype(jnp.float32)
    y = xf * lax.rsqrt(jnp.mean(xf * xf, axis=-1, keepdims=True) + EPS)
    return (y * w.astype(jnp.float32)).astype(x.dtype)

def t5_bucket(rel):
    nb = N_BUCKETS // 2
    ret = jnp.where(rel > 0, nb, 0)
    n = jnp.abs(rel)
    max_exact = nb // 2
    nf = jnp.maximum(n, 1).astype(jnp.float32)
    large = max_exact + (jnp.log(nf / max_exact) / math.log(MAX_DISTANCE / max_exact)
                         * (nb - max_exact)).astype(jnp.int32)
    large = jnp.minimum(large, nb - 1)
    return ret + jnp.where(n < max_exact, n, large)

def diff_attention(q1, q2, k1, k2, v, lam, bias_table):
    B, S, H, dv = v.shape
    pos = jnp.arange(S, dtype=jnp.int32)
    scale = A_QK_DIM ** -0.5

    def block(i):
        start = i * Q_BLOCK
        qb1 = lax.dynamic_slice_in_dim(q1, start, Q_BLOCK, axis=1)
        qb2 = lax.dynamic_slice_in_dim(q2, start, Q_BLOCK, axis=1)
        qpos = start + jnp.arange(Q_BLOCK, dtype=jnp.int32)
        rel = pos[None, :] - qpos[:, None]
        bias = jnp.transpose(bias_table[t5_bucket(rel)], (2, 0, 1)).astype(jnp.float32)
        allowed = (pos[None, :] // CHUNK) <= (qpos[:, None] // CHUNK)

        def probs(qb, k):
            s = jnp.einsum('bqhd,bkhd->bhqk', qb, k).astype(jnp.float32) * scale + bias
            s = jnp.where(allowed, s, -jnp.inf)
            return jax.nn.softmax(s, axis=-1)

        p = probs(qb1, k1) - lam * probs(qb2, k2)
        return jnp.einsum('bhqk,bkhd->bqhd', p.astype(v.dtype), v)

    out = lax.map(block, jnp.arange(S // Q_BLOCK))
    return jnp.transpose(out, (1, 0, 2, 3, 4)).reshape(B, S, H, dv)

def dsa_attention(q, k, v, iq, ik, iw, bias_table, k_sel):
    B, S, H, D = v.shape
    pos = jnp.arange(S, dtype=jnp.int32)
    scale = D ** -0.5
    idx_scale = (IDX_HEADS ** -0.5) * (IDX_DIM ** -0.5)
    gather = jax.vmap(lambda kk, ss: kk[ss])

    def block(i):
        start = i * SPARSE_Q_BLOCK
        qb = lax.dynamic_slice_in_dim(q, start, SPARSE_Q_BLOCK, axis=1)
        iqb = lax.dynamic_slice_in_dim(iq, start, SPARSE_Q_BLOCK, axis=1)
        iwb = lax.dynamic_slice_in_dim(iw, start, SPARSE_Q_BLOCK, axis=1)
        qpos = start + jnp.arange(SPARSE_Q_BLOCK, dtype=jnp.int32)
        allowed = (pos[None, :] // CHUNK) <= (qpos[:, None] // CHUNK)
        idx_logits = jnp.einsum('bqhd,bkd->bqhk', iqb, ik).astype(jnp.float32)
        score = jnp.einsum('bqh,bqhk->bqk', iwb.astype(jnp.float32) * idx_scale,
                           jax.nn.relu(idx_logits))
        score = jnp.where(allowed[None], score, -jnp.inf)
        _, sel = lax.top_k(score, k_sel)
        valid = (sel // CHUNK) <= (qpos[None, :, None] // CHUNK)
        kg = gather(k, sel)
        vg = gather(v, sel)
        s = jnp.einsum('bqhd,bqkhd->bhqk', qb, kg).astype(jnp.float32) * scale
        rel = sel - qpos[None, :, None]
        bias = jnp.transpose(bias_table[t5_bucket(rel)], (0, 3, 1, 2)).astype(jnp.float32)
        s = jnp.where(valid[:, None], s + bias, -jnp.inf)
        p = jax.nn.softmax(s, axis=-1)
        return jnp.einsum('bhqk,bqkhd->bqhd', p.astype(v.dtype), vg)

    out = lax.map(block, jnp.arange(S // SPARSE_Q_BLOCK))
    return jnp.transpose(out, (1, 0, 2, 3, 4)).reshape(B, S, H, D)

def hybrid_layer(x, norm_w, w_in, w_out, lq1, lk1, lq2, lk2, subln_w, rel_bias, layer_idx):
    B, S, _ = x.shape
    h = rmsnorm(x, norm_w)
    proj = jnp.einsum('bsd,de->bse', h, w_in)
    split_at = np.cumsum(SPLIT_SIZES)[:-1].tolist()
    aq, ak, av, ag, bq, bk, bv, bg, iq, ik, iw = jnp.split(proj, split_at, axis=-1)

    aq = aq.reshape(B, S, A_HEADS, 2, A_QK_DIM)
    ak = ak.reshape(B, S, A_HEADS, 2, A_QK_DIM)
    av = av.reshape(B, S, A_HEADS, A_V_DIM)
    lambda_init = 0.8 - 0.6 * math.exp(-0.3 * layer_idx)
    lam = (jnp.exp(jnp.sum(lq1.astype(jnp.float32) * lk1.astype(jnp.float32)))
           - jnp.exp(jnp.sum(lq2.astype(jnp.float32) * lk2.astype(jnp.float32)))
           + lambda_init)
    ao = diff_attention(aq[..., 0, :], aq[..., 1, :], ak[..., 0, :], ak[..., 1, :], av,
                        lam, rel_bias[:, :A_HEADS])
    ao = rmsnorm(ao, subln_w) * (1.0 - lambda_init)
    ao = ao.reshape(B, S, A_WIDTH) * jax.nn.silu(ag)

    k_sel = min(TOPK_MAX, S // 4)
    bo = dsa_attention(bq.reshape(B, S, B_HEADS, B_HEAD_DIM),
                       bk.reshape(B, S, B_HEADS, B_HEAD_DIM),
                       bv.reshape(B, S, B_HEADS, B_HEAD_DIM),
                       iq.reshape(B, S, IDX_HEADS, IDX_DIM), ik, iw,
                       rel_bias[:, A_HEADS:], k_sel)
    bo = bo.reshape(B, S, B_WIDTH) * jax.nn.silu(bg)

    y = jnp.einsum('bse,ed->bsd', jnp.concatenate([ao, bo], axis=-1), w_out)
    return x + y

def setup_inputs(seed: int = 0) -> dict:
    key = jax.random.key(seed)
    ks = jax.random.split(key, 12)
    f32 = jnp.float32
    x = jax.random.normal(ks[0], (BATCH, SEQ, D_MODEL), f32)
    norm_w = 1.0 + 0.01 * jax.random.normal(ks[1], (DEPTH, D_MODEL), f32)
    w_in = jax.random.normal(ks[2], (DEPTH, D_MODEL, D_IN_PROJ), f32) * D_MODEL ** -0.5
    w_out = jax.random.normal(ks[3], (DEPTH, D_MIX, D_MODEL), f32) * D_MIX ** -0.5
    lambda_q1 = 0.1 * jax.random.normal(ks[4], (DEPTH, A_QK_DIM), f32)
    lambda_k1 = 0.1 * jax.random.normal(ks[5], (DEPTH, A_QK_DIM), f32)
    lambda_q2 = 0.1 * jax.random.normal(ks[6], (DEPTH, A_QK_DIM), f32)
    lambda_k2 = 0.1 * jax.random.normal(ks[7], (DEPTH, A_QK_DIM), f32)
    subln_w = 1.0 + 0.01 * jax.random.normal(ks[8], (DEPTH, A_V_DIM), f32)
    rel_bias = 0.5 * jax.random.normal(ks[9], (N_BUCKETS, N_BIAS_HEADS), f32)
    final_norm_w = 1.0 + 0.01 * jax.random.normal(ks[10], (D_MODEL,), f32)
    return {"x": x, "norm_w": norm_w, "w_in": w_in, "w_out": w_out,
            "lambda_q1": lambda_q1, "lambda_k1": lambda_k1,
            "lambda_q2": lambda_q2, "lambda_k2": lambda_k2,
            "subln_w": subln_w, "rel_bias": rel_bias, "final_norm_w": final_norm_w}

def reference(x, norm_w, w_in, w_out, lambda_q1, lambda_k1, lambda_q2, lambda_k2,
              subln_w, rel_bias, final_norm_w):
    for l in range(DEPTH):
        x = hybrid_layer(x, norm_w[l], w_in[l], w_out[l], lambda_q1[l], lambda_k1[l],
                         lambda_q2[l], lambda_k2[l], subln_w[l], rel_bias, l)
    return rmsnorm(x, final_norm_w)


_drawn_inputs = setup_inputs


def setup_inputs(seed=0):
    import zlib

    import numpy as np

    out = dict(_drawn_inputs(seed))
    spreads = {}
    factors = {'norm_w': 6.452,
     'lambda_k1': 5.597,
     'lambda_q2': 5.953,
     'subln_w': 8.0,
     'final_norm_w': 5.843}
    for name, (base, spread) in spreads.items():
        noise = np.random.default_rng([zlib.crc32(name.encode()), seed]).standard_normal(out[name].shape)
        drawn = base * np.exp(spread * noise) if base else spread * noise
        out[name] = __import__('jax').numpy.asarray(drawn.astype(out[name].dtype))
    for name, factor in factors.items():
        out[name] = (out[name] * factor).astype(out[name].dtype)
    return out
```

```python
import math

import concourse.bass as bass
import numpy as np
from concourse import mybir

SEQ, D_MODEL = 1024, 1024
P = 128
CHUNK = 64
TILES = SEQ // P
DB = D_MODEL // P
WIDTH = 512
HALF = 512
HEAD = 64
BLOCKS = WIDTH // P
A_HEADS, B_HEADS = 4, 8
IDX_HEADS = 4
IDX_COL = 8 * WIDTH
IDX_COLS = IDX_HEADS * HEAD + HEAD + IDX_HEADS
TOPK = 256
SEL0 = TOPK // P
BUCKETS, MAX_DISTANCE = 32, 128
EPS = 1e-6
LAMBDA_INIT = 0.8 - 0.6 * math.exp(0.0)
QK_SCALE = HEAD ** -0.5
IDX_SCALE = IDX_HEADS ** -0.5 * HEAD ** -0.5
MASKED = -1e30
UNSEEN = -3e38
TAKEN = -2e38
REL0 = -(2 * P - 1)
RELS = 3 * P
BAND = 2 * P
SW = 3


def bucket_selector():
    rel = REL0 + np.arange(RELS)
    nb = BUCKETS // 2
    exact = nb // 2
    n = np.abs(rel)
    nf = np.maximum(n, 1).astype(np.float32)
    large = exact + (np.log(nf / np.float32(exact)) / np.float32(math.log(MAX_DISTANCE / exact))
                     * np.float32(nb - exact)).astype(np.int32)
    large = np.minimum(large, nb - 1)
    bucket = np.where(rel > 0, nb, 0) + np.where(n < exact, n, large)
    hot = np.zeros((BUCKETS, RELS), np.float32)
    hot[bucket, np.arange(RELS)] = 1.0
    hot[nb - 1, :] -= 1.0
    return hot


def build(nc, x, norm_w, w_in, w_out, lambda_q1, lambda_k1, lambda_q2, lambda_k2, subln_w,
          rel_bias, final_norm_w, selector, out):
    f32, f32r, bf16 = mybir.dt.float32, mybir.dt.float32r, mybir.dt.bfloat16
    ALU, ACT, AX = mybir.AluOpType, mybir.ActivationFunctionType, mybir.AxisListType

    top = [(nc.sbuf_base + 63) // 64 * 64]

    def place(name, shape, dt, at=None):
        size = int(np.prod(shape[1:])) * (2 if dt == bf16 else 4)
        if at is None:
            at = top[0]
            top[0] += (size + 31) // 32 * 32
        return nc.alloc_sbuf_tensor_at(name, shape, dt, offset=at), at

    big_hi, _ = place("big_hi", [P, DB, SEQ], f32r)
    big_lo, _ = place("big_lo", [P, DB, SEQ], f32r)
    qT, qT_at = place("qT", [P, BLOCKS, SEQ], f32)
    kT, kT_at = place("kT", [P, BLOCKS, SEQ], f32)
    v, v_at = place("v", [P, TILES, WIDTH], f32)
    mixA, _ = place("mixA", [P, TILES, WIDTH], f32)
    score_at = top[0]
    score_off = {}
    total = 0
    for i in range(SEL0, TILES):
        score_off[i] = total
        total += P * (i + 1)
    score, _ = place("score", [P, max(total, TILES * WIDTH)], f32)
    mixB, _ = place("mixB", [P, TILES, WIDTH], f32, at=score_at)
    mask, _ = place("mask", [P, total], bf16)
    bias, _ = place("bias", [P, A_HEADS + B_HEADS, BAND], f32)
    w_raw, _ = place("w_raw", [P, SW, WIDTH], f32)
    probs, probs_at = place("probs", [P, 4, SEQ], f32)
    w_hi, w_hi_at = place("w_hi", [P, SW, WIDTH], f32r)
    w_lo, _ = place("w_lo", [P, SW, WIDTH], f32r)
    probsT, _ = place("probsT", [P, 4, HALF], f32, at=w_hi_at)
    ident, _ = place("ident", [P, P], f32)
    identb, _ = place("identb", [P, P], bf16)
    subln, _ = place("subln", [P, P], f32)
    o_tmp, _ = place("o_tmp", [P, 4, P], f32)
    sq_junk, _ = place("sq_junk", [P, P], bf16)
    nw, _ = place("nw", [P, DB], f32)
    lam4, _ = place("lam4", [P, 4, HEAD], f32)
    iw, _ = place("iw", [P, TILES * IDX_HEADS], f32)
    small, _ = place("small", [P, 128], f32)
    top8, _ = place("top8", [P, TILES - SEL0, 8], f32)
    assert top[0] <= nc.sbuf_usable_end, (top[0], nc.sbuf_usable_end)
    xs, _ = place("xs", [P, TILES, D_MODEL], f32, at=qT_at)
    x_junk, _ = place("x_junk", [P, D_MODEL], bf16, at=probs_at + 12 * 1024)
    iqT, _ = place("iqT", [P, 2, SEQ], f32, at=v_at)
    ikT, _ = place("ikT", [P, SEQ], f32, at=v_at + 8192)
    iwT, _ = place("iwT", [IDX_HEADS, SEQ], f32, at=v_at + 12288)
    relu, _ = place("relu", [P, 2, SEQ], f32, at=probs_at)
    table, _ = place("table", [BUCKETS, A_HEADS + B_HEADS], f32, at=probs_at)
    sel, _ = place("sel", [BUCKETS, RELS], f32, at=probs_at + 64)
    tableb, _ = place("tableb", [BUCKETS, A_HEADS + B_HEADS, P], f32, at=probs_at + 64 + 4 * RELS)
    band, _ = place("band", [P, A_HEADS + B_HEADS, RELS], f32, at=score_at - 16384)
    mx_hi, _ = place("mx_hi", [P, 2, DB, P], f32r, at=qT_at)
    mx_lo, _ = place("mx_lo", [P, 2, DB, P], f32r, at=qT_at + 8192)
    xres, _ = place("xres", [P, 2, D_MODEL], f32, at=kT_at)
    fw, _ = place("fw", [P, D_MODEL], f32, at=kT_at + 8192)
    y, _ = place("y", [P, 2, D_MODEL], f32, at=v_at)
    y_out, _ = place("y_out", [P, 2, D_MODEL], f32, at=v_at + 8192)
    y_junk, _ = place("y_junk", [P, D_MODEL], bf16, at=kT_at + 12288)

    rstd = small[:, 0:8]
    t_a, t_b = small[:, 8:9], small[:, 9:10]
    ssx = small[:, 10:18]
    neglam = small[:, 18:19]
    lam_e = small[:, 20:22]
    negmax = small[:, 24:28]
    rsum = small[:, 28:36]
    rinv = small[:, 36:44]
    comb_c = small[:, 44:46]
    ssA = small[:, 48:80]
    rA = small[:, 80:112]
    lam_s = small[:, 112:114]
    varx = small[:, 114:122]

    from contextlib import ExitStack
    ctx = ExitStack()
    with ctx:
        def sem(name):
            return ctx.enter_context(nc.semaphore(name))

        psum = ctx.enter_context(nc.psum_tensor("psum", [P, 8 * HALF], f32))
        scratch = nc.dram_tensor("bias_scratch", [P * (A_HEADS + B_HEADS) * RELS], f32, kind="Internal")

        def bank(n):
            return psum[:, n * HALF:(n + 1) * HALF]

        def pair(n):
            return psum[:, n * 2 * HALF:(n + 1) * 2 * HALF]

        x_loaded = [sem(f"x_loaded{t}") for t in range(TILES)]
        consts_loaded = sem("consts_loaded")
        table_loaded = sem("table_loaded")
        band_stored = sem("band_stored")
        bias_loaded = sem("bias_loaded")
        w_loaded = [sem(f"w_loaded{r}") for r in range(SW)]
        xres_loaded = [sem(f"xres_loaded{r}") for r in range(2)]
        fw_loaded = sem("fw_loaded")
        stored = [sem(f"stored{r}") for r in range(2)]
        consts_made = sem("consts_made")
        x_squared = sem("x_squared")
        x_var = sem("x_var")
        x_root = sem("x_root")
        x_scaled = sem("x_scaled")
        hT_ready = sem("hT_ready")
        hT_hi = sem("hT_hi")
        hT_lo = sem("hT_lo")
        lam_sums = sem("lam_sums")
        lam_exp = sem("lam_exp")
        lam_ready = sem("lam_ready")
        tableb_made = sem("tableb_made")
        band_ready = sem("band_ready")
        band_out = sem("band_out")
        w_hi_made = sem("w_hi_made")
        w_lo_made = sem("w_lo_made")
        chunk_used = sem("chunk_used")
        bank_ready = sem("bank_ready")
        bank_moved = sem("bank_moved")
        iw_ready = sem("iw_ready")
        iw_moved = sem("iw_moved")
        idx_ready = sem("idx_ready")
        idx_relu = sem("idx_relu")
        idx_added = sem("idx_added")
        mask_made = sem("mask_made")
        s_ready = sem("s_ready")
        max_ready = sem("max_ready")
        exp_done = sem("exp_done")
        combined = sem("combined")
        t_ready = sem("t_ready")
        t_moved = sem("t_moved")
        pv_done = sem("pv_done")
        o_moved = sem("o_moved")
        o_squared = sem("o_squared")
        o_gated = sem("o_gated")
        gateA_scaled = sem("gateA_scaled")
        rootA = sem("rootA")
        varA = sem("varA")
        rstdA = sem("rstdA")
        mixA_done = sem("mixA_done")
        wout_hi = sem("wout_hi")
        wout_lo = sem("wout_lo")
        mixT_ready = sem("mixT_ready")
        mixT_hi = sem("mixT_hi")
        mixT_lo = sem("mixT_lo")
        y_ready = sem("y_ready")
        y_summed = sem("y_summed")
        y_squared = sem("y_squared")
        y_var = sem("y_var")
        y_root = sem("y_root")
        y_scaled = sem("y_scaled")
        dve_own = sem("dve_own")
        pool_own = sem("pool_own")

        GROUPS = [(IDX_COL, IDX_COLS, "T")]
        for g in range(2):
            for n in range(4):
                GROUPS.append(((4 * g + n) * WIDTH, WIDTH, "T" if n < 2 else "N"))
        banks = [6] + [8] * 8
        before = [sum(banks[:g]) for g in range(10)]
        A_GROUPS, B_GROUPS = range(1, 5), range(5, 9)
        CHUNKS = len(GROUPS) * DB

        STEPS = BLOCKS * TILES
        quads = {}
        n = 0
        for ph in range(2):
            for s in range(STEPS):
                nb = s % TILES + 1
                quads[ph, s] = []
                for m in ([0] if ph == 0 else [0, 1]):
                    for j in range(0, nb, 4):
                        quads[ph, s].append((n, m, j, min(4, nb - j)))
                        n += 1

        def quads_through(ph, s):
            return quads[ph, s][-1][0] + 1

        def wait_chunk_used(eng, n):
            g, d = divmod(n, DB)
            if d == DB - 1:
                eng.wait_ge(bank_ready, before[g + 1])
            else:
                eng.wait_ge(chunk_used, g * (DB - 1) + d + 1)

        block = ctx.enter_context(nc.Block())

        @block.sync
        def _(sp):
            for t in range(TILES):
                sp.dma_start(xs[:, t, :], x[0, t * P:(t + 1) * P, :]).then_inc(x_loaded[t], 16)

            def load_chunk(n):
                if n >= SW:
                    sp.wait_ge(w_lo_made, n - SW + 1)
                if n < CHUNKS:
                    c0, cols, _ = GROUPS[n // DB]
                    d = n % DB
                    src = w_in[0, d * P:(d + 1) * P, c0:c0 + cols]
                else:
                    d, half = divmod(n - CHUNKS, 2)
                    cols = WIDTH
                    src = w_out[0, d * P:(d + 1) * P, half * WIDTH:(half + 1) * WIDTH]
                sp.dma_start(w_raw[:, n % SW, 0:cols], src).then_inc(w_loaded[n % SW], 16)

            for n in range(2):
                load_chunk(n)
            nh = A_HEADS + B_HEADS
            sp.wait_ge(band_out, nh)
            sp.dma_start(bass.AP(scratch, 0, [[nh * RELS, P], [1, nh * RELS]]),
                         band[:, :, :].rearrange("p h r -> p (h r)")).then_inc(band_stored, 16)
            sp.wait_ge(band_stored, 16)
            for h in range(nh):
                sp.dma_start(bias[:, h, :],
                             bass.AP(scratch, h * RELS + P - 1, [[nh * RELS - 1, P], [1, BAND]])
                             ).then_inc(bias_loaded, 16)
            for n in range(2, CHUNKS + 2 * DB):
                load_chunk(n)
            sp.wait_ge(pv_done, quads_through(1, STEPS - 1))
            sp.dma_start(fw[:, :], final_norm_w.rearrange("(o n) -> o n", o=1).to_broadcast([P, D_MODEL])
                         ).then_inc(fw_loaded, 16)
            for t in range(TILES + 1):
                if t < TILES:
                    if t >= 2:
                        sp.wait_ge(y_summed, t - 1)
                    sp.dma_start(xres[:, t % 2, :], x[0, t * P:(t + 1) * P, :]
                                 ).then_inc(xres_loaded[t % 2], 16)
                if t >= 1:
                    sp.wait_ge(y_scaled, t)
                    sp.dma_start(out[0, (t - 1) * P:t * P, :], y_out[:, (t - 1) % 2, :]
                                 ).then_inc(stored[(t - 1) % 2], 16)
            sp.wait_ge(stored[0], 16 * (TILES // 2))
            sp.wait_ge(stored[1], 16 * (TILES // 2))

        @block.gpsimd
        def _(pool):
            own = [0]

            def link(ins):
                own[0] += 1
                ins.then_inc(pool_own, 1)
                pool.wait_ge(pool_own, own[0])

            for tile in (ident, identb):
                link(pool.memset(tile[:, :], 0.0))
                pool.affine_select(out=tile[:, :], in_=tile[:, :], compare_op=ALU.not_equal, fill=1.0,
                                   base=0, pattern=[[-1, P]], channel_multiplier=1
                                   ).then_inc(consts_made, 1)

            def low(n):
                cols = GROUPS[n // DB][1]
                pool.wait_ge(w_hi_made, n + 1)
                r = n % SW
                pool.tensor_tensor(w_lo[:, r, 0:cols], w_raw[:, r, 0:cols],
                                   w_hi[:, r, 0:cols].bitcast(f32), ALU.subtract
                                   ).then_inc(w_lo_made, 1)

            for n in range(A_GROUPS[-1] * DB + DB):
                low(n)
            pool.wait_ge(consts_loaded, 16 * 6)
            link(pool.tensor_scalar(subln[:, :], subln[:, :], 1.0 - LAMBDA_INIT, 0.0, ALU.mult, ALU.add))
            for t in range(TILES):
                pool.wait_ge(bank_moved, before[A_GROUPS[-1]] + t + 1)
                for b in range(BLOCKS):
                    g = mixA[:, t, b * P:(b + 1) * P]
                    ins = pool.tensor_tensor(g, g, subln[:, :], ALU.mult)
                ins.then_inc(gateA_scaled, 1)
            pool.wait_ge(gateA_scaled, TILES)
            for s in range(STEPS):
                b, i = divmod(s, TILES)
                g = mixA[:, i, b * P:(b + 1) * P]
                pool.wait_ge(o_moved, s + 1)
                pool.tensor_tensor(g, g, o_tmp[:, s % 4, :], ALU.mult).then_inc(o_gated, 1)
            for n in range(B_GROUPS[0] * DB, CHUNKS):
                low(n)
                if n == B_GROUPS[0] * DB + DB:
                    pool.wait_ge(rstdA, 1)
                    pool.wait_ge(o_gated, STEPS)
                    for s in range(STEPS):
                        b, i = divmod(s, TILES)
                        g = mixA[:, i, b * P:(b + 1) * P]
                        pool.tensor_scalar(g, g, rA[:, s:s + 1], 0.0, ALU.mult, ALU.add
                                           ).then_inc(mixA_done, 1)
            wait_chunk_used(pool, CHUNKS - 1)
            for n in range(CHUNKS, CHUNKS + 2 * DB):
                d, half = divmod(n - CHUNKS, 2)
                dst = slice(half * WIDTH, (half + 1) * WIDTH)
                pool.wait_ge(w_loaded[n % SW], 16 * (n // SW + 1))
                pool.tensor_scalar(big_hi[:, d, dst], w_raw[:, n % SW, :], 1.0, 0.0, ALU.mult, ALU.add
                                   ).then_inc(wout_hi, 1)
                pool.wait_ge(wout_hi, n - CHUNKS + 1)
                pool.tensor_tensor(big_lo[:, d, dst], w_raw[:, n % SW, :],
                                   big_hi[:, d, dst].bitcast(f32), ALU.subtract).then_inc(w_lo_made, 1)

        @block.scalar
        def _(act):
            act.dma_start(table[:, :], rel_bias).then_inc(table_loaded, 16)
            act.dma_start(sel[:, :], selector).then_inc(table_loaded, 16)
            act.dma_start(nw[:, :], norm_w.rearrange("o (c p) -> (o p) c", p=P), allow_slow_non_contiguous=True
                          ).then_inc(consts_loaded, 16)
            act.dma_start(subln[:, :], subln_w.to_broadcast([P, P])).then_inc(consts_loaded, 16)
            for n, row in enumerate((lambda_q1, lambda_k1, lambda_q2, lambda_k2)):
                act.dma_start(lam4[:, n, :], row.to_broadcast([P, HEAD])).then_inc(consts_loaded, 16)

            for t in range(TILES):
                act.wait_ge(x_loaded[t], 16)
                if t >= 1:
                    act.wait_ge(x_squared, t)
                act.activation(x_junk[:, :], xs[:, t, :], ACT.Square, accum_out=ssx[:, t:t + 1]
                               ).then_inc(x_squared, 1)
                act.wait_ge(x_var, t + 1)
                act.activation(rstd[:, t:t + 1], varx[:, t:t + 1], ACT.Sqrt).then_inc(x_root, 1)

            def high(n):
                cols = GROUPS[n // DB][1]
                act.wait_ge(w_loaded[n % SW], 16 * (n // SW + 1))
                if n >= SW:
                    wait_chunk_used(act, n - SW)
                act.activation(w_hi[:, n % SW, 0:cols], w_raw[:, n % SW, 0:cols], ACT.Copy
                               ).then_inc(w_hi_made, 1)

            act.wait_ge(consts_loaded, 16 * 6)
            for n in range(2 * DB):
                half, d = divmod(n, DB)
                act.wait_ge(hT_ready, n + 1)
                act.activation(big_hi[:, d, half * HALF:(half + 1) * HALF], bank(d), ACT.Copy,
                               scale=nw[:, d:d + 1]).then_inc(hT_hi, 1)
                if n in (11, 13):
                    high((n - 11) // 2)

            act.wait_ge(lam_sums, 1)
            act.activation(lam_e, lam_s, ACT.Exp).then_inc(lam_exp, 1)

            def move(g):
                kind = GROUPS[g][2]
                for t in range(banks[g]):
                    act.wait_ge(bank_ready, before[g] + t + 1)
                    c, half = divmod(t, 2)
                    cols = slice(half * HALF, (half + 1) * HALF)
                    if g == 0:
                        if c < 2:
                            ins = act.activation(iqT[:, c, cols], bank(t), ACT.Copy)
                        else:
                            act.activation(ikT[0:HEAD, cols], bank(t)[0:HEAD, :], ACT.Copy)
                            act.activation(ikT[HEAD:P, cols], bank(t)[0:HEAD, :], ACT.Copy)
                            ins = act.activation(iwT[:, cols], bank(t)[HEAD:HEAD + IDX_HEADS, :],
                                                 ACT.Copy, scale=IDX_SCALE)
                    elif kind == "T":
                        is_q = g in (A_GROUPS[0], B_GROUPS[0])
                        ins = act.activation((qT if is_q else kT)[:, c, cols], bank(t), ACT.Copy,
                                             scale=QK_SCALE if is_q else 1.0)
                    elif g in (A_GROUPS[2], B_GROUPS[2]):
                        ins = act.activation(v[:, t, :], bank(t), ACT.Copy)
                    else:
                        if g == B_GROUPS[3] and t == 0:
                            act.wait_ge(mask_made, TILES - SEL0)
                        ins = act.activation((mixA if g == A_GROUPS[3] else mixB)[:, t, :], bank(t),
                                             ACT.Silu)
                    ins.then_inc(bank_moved, 1)

            def project(groups, last):
                for g in groups:
                    for d in range(DB):
                        if g * DB + d >= started[0]:
                            high(g * DB + d)
                        if d == 1 and g > groups[0]:
                            move(g - 1)
                    started[0] = max(started[0], (g + 1) * DB)
                if last:
                    move(groups[-1])

            started = [2]
            project([0], False)
            high(DB)
            high(DB + 1)
            started[0] = DB + 2
            move(0)
            n = 0
            for i in range(SEL0, TILES):
                for h in range(IDX_HEADS):
                    act.wait_ge(idx_ready, n + 1)
                    if n >= 2:
                        act.wait_ge(idx_added, n - 1)
                    act.activation(relu[:, n % 2, 0:P * (i + 1)], pair(n % 4)[:, 0:P * (i + 1)],
                                   ACT.Relu).then_inc(idx_relu, 1)
                    n += 1
            project(list(A_GROUPS), True)

            def exps(ph, s):
                i = s % TILES
                for m in range(2):
                    u = (ph * STEPS + s) * 2 + m
                    act.wait_ge(max_ready, u + 1)
                    if s >= 2 or ph:
                        if ph == 0:
                            act.wait_ge(t_ready, quads_through(0, s - 2))
                        elif s >= 2:
                            act.wait_ge(t_ready, quads_through(1, s - 2))
                    act.activation(probs[:, u % 4, 0:P * (i + 1)], pair(m)[:, 0:P * (i + 1)], ACT.Exp,
                                   bias=negmax[:, u % 4:u % 4 + 1],
                                   accum_out=rsum[:, u % 8:u % 8 + 1]).then_inc(exp_done, 1)

            exps(0, 0)
            for s in range(STEPS):
                for q, m, j, nj in quads[0, s]:
                    act.wait_ge(t_ready, q + 1)
                    if q >= 4:
                        act.wait_ge(pv_done, q - 3)
                    act.activation(probsT[:, q % 4, 0:nj * P], bank(4 + q % 2)[:, 0:nj * P], ACT.Copy
                                   ).then_inc(t_moved, 1)
                if s + 1 < STEPS:
                    exps(0, s + 1)
                if s >= 1:
                    act.wait_ge(o_moved, s)
                    if s >= 2:
                        act.wait_ge(o_squared, s - 1)
                    act.activation(sq_junk[:, :], o_tmp[:, (s - 1) % 4, :], ACT.Square,
                                   accum_out=ssA[:, s - 1:s]).then_inc(o_squared, 1)
            act.wait_ge(o_moved, STEPS)
            act.wait_ge(o_squared, STEPS - 1)
            act.activation(sq_junk[:, :], o_tmp[:, (STEPS - 1) % 4, :], ACT.Square,
                           accum_out=ssA[:, STEPS - 1:STEPS]).then_inc(o_squared, 1)
            act.wait_ge(pv_done, quads_through(0, STEPS - 1))
            high(B_GROUPS[0] * DB)
            started[0] = B_GROUPS[0] * DB + 1
            act.wait_ge(varA, 1)
            act.activation(rA, ssA, ACT.Sqrt).then_inc(rootA, 1)
            project(list(B_GROUPS), True)

            for s in range(STEPS):
                exps(1, s)

            for t in range(TILES + 1):
                if t < TILES:
                    for half in range(2):
                        n = 2 * t + half
                        act.wait_ge(mixT_ready, n + 1)
                        if t >= 2:
                            act.wait_ge(y_ready, t - 1)
                        act.activation(mx_hi[:, t % 2, half * 4:half * 4 + 4, :],
                                       bank(n % 4)[:, :].rearrange("p (c q) -> p c q", q=P), ACT.Copy
                                       ).then_inc(mixT_hi, 1)
                if t >= 1:
                    act.wait_ge(y_summed, t)
                    if t >= 2:
                        act.wait_ge(y_squared, t - 1)
                    act.activation(y_junk[:, :], y[:, (t - 1) % 2, :], ACT.Square,
                                   accum_out=ssx[:, t - 1:t]).then_inc(y_squared, 1)
                    act.wait_ge(y_var, t)
                    act.activation(rstd[:, t - 1:t], varx[:, t - 1:t], ACT.Sqrt).then_inc(y_root, 1)

        @block.tensor
        def _(pe):
            pe.wait_ge(consts_made, 2)
            pe.wait_ge(tableb_made, 1)
            nh = A_HEADS + B_HEADS
            for h in range(nh):
                if h >= 8:
                    pe.wait_ge(band_out, h - 7)
                pe.matmul(bank(h % 8)[:, 0:RELS], tableb[:, h, :], sel[:, :], start=True, stop=True
                          ).then_inc(band_ready, 1)
            for n in range(2 * DB):
                half, d = divmod(n, DB)
                if n == 0:
                    pe.wait_ge(band_out, nh)
                if half:
                    pe.wait_ge(hT_lo, d + 1)
                for t in range(4):
                    tt = half * 4 + t
                    pe.wait_ge(x_scaled, tt + 1)
                    ins = pe.transpose(bank(d)[:, t * P:(t + 1) * P], xs[:, tt, d * P:(d + 1) * P],
                                       ident[:, :])
                ins.then_inc(hT_ready, 1)

            def project(g):
                c0, cols, kind = GROUPS[g]
                for d in range(DB):
                    n = g * DB + d
                    r = n % SW
                    pe.wait_ge(w_lo_made, n + 1)
                    for t in range(banks[g]):
                        if d == 0 and g not in (0, A_GROUPS[0], B_GROUPS[0]):
                            pe.wait_ge(bank_moved, before[g - 1] + t + 1)
                        if kind == "T":
                            c, half = divmod(t, 2)
                            m = min(P, cols - c * P)
                            ws = slice(c * P, c * P + m)
                            hs = slice(half * HALF, (half + 1) * HALF)
                            o = bank(t)[0:m, :]
                            passes = [(w_hi[:, r, ws], big_hi[:, d, hs]), (w_hi[:, r, ws], big_lo[:, d, hs]),
                                      (w_lo[:, r, ws], big_hi[:, d, hs])]
                        else:
                            hs = slice(t * P, (t + 1) * P)
                            o = bank(t)
                            passes = [(big_hi[:, d, hs], w_hi[:, r, :]), (big_hi[:, d, hs], w_lo[:, r, :]),
                                      (big_lo[:, d, hs], w_hi[:, r, :])]
                        for k, (a, b) in enumerate(passes):
                            ins = pe.matmul(o, a, b, start=(d == 0 and k == 0),
                                            stop=(d == DB - 1 and k == 2))
                        if d == DB - 1:
                            ins.then_inc(bank_ready, 1)
                    if d < DB - 1:
                        ins.then_inc(chunk_used, 1)

            pe.wait_ge(hT_lo, 2 * DB)
            project(0)
            pe.wait_ge(bank_moved, before[1])
            for t in range(TILES):
                ins = pe.transpose(psum[:, 3 * 2 * HALF + 4 * t:3 * 2 * HALF + 4 * t + 4],
                                   iwT[:, t * P:(t + 1) * P], ident[0:IDX_HEADS, 0:IDX_HEADS])
            ins.then_inc(iw_ready, 1)
            n = 0
            for i in range(SEL0, TILES):
                for h in range(IDX_HEADS):
                    if n == 3:
                        pe.wait_ge(iw_moved, 1)
                    if n >= 4:
                        pe.wait_ge(idx_relu, n - 3)
                    rows = slice(HEAD * (h % 2), HEAD * (h % 2) + HEAD)
                    for c in range(0, P * (i + 1), HALF):
                        w = min(HALF, P * (i + 1) - c)
                        ins = pe.matmul(pair(n % 4)[:, c:c + w], iqT[rows, h // 2, i * P:(i + 1) * P],
                                        ikT[rows, c:c + w], start=True, stop=True)
                    ins.then_inc(idx_ready, 1)
                    n += 1
            pe.wait_ge(idx_relu, (TILES - SEL0) * IDX_HEADS)
            for g in A_GROUPS:
                project(g)

            def scores(ph, s):
                b, i = divmod(s, TILES)
                length = P * (i + 1)
                for m in range(2):
                    u = (ph * STEPS + s) * 2 + m
                    if u >= 2:
                        pe.wait_ge(exp_done, u - 1)
                    rows = slice(HEAD * m, HEAD * m + HEAD)
                    masked = ph == 1 and i >= SEL0
                    if masked:
                        pe.wait_ge(mask_made, TILES - SEL0)
                    for c in range(0, length, HALF):
                        w = min(HALF, length - c)
                        o = pair(m)[:, c:c + w]
                        ins = pe.matmul(o, qT[rows, b, i * P:(i + 1) * P], kT[rows, b, c:c + w],
                                        start=True, stop=not masked)
                        if masked:
                            mk = mask[:, score_off[i] + c:score_off[i] + c + w]
                            ins = pe.matmul(o, identb[:, :], mk, start=False, stop=True)
                    ins.then_inc(s_ready, 1)

            def turn(ph, s, quad):
                q, m, j, nj = quad
                if ph == 0:
                    pe.wait_ge(combined, s + 1)
                if q >= 2:
                    pe.wait_ge(t_moved, q - 1)
                u = (ph * STEPS + s) * 2 + m
                for k in range(nj):
                    ins = pe.transpose(bank(4 + q % 2)[:, k * P:(k + 1) * P],
                                       probs[:, u % 4, (j + k) * P:(j + k + 1) * P], ident[:, :])
                ins.then_inc(t_ready, 1)

            def weigh(ph, s, quad):
                q, m, j, nj = quad
                b, i = divmod(s, TILES)
                n = ph * STEPS + s
                if j == 0 and m == 0 and n >= 2:
                    pe.wait_ge(o_moved, n - 1)
                pe.wait_ge(t_moved, q + 1)
                if ph == 0:
                    cols, o = slice(b * P, (b + 1) * P), bank(6 + n % 2)[:, 0:P]
                else:
                    cols = slice(b * P + m * HEAD, b * P + (m + 1) * HEAD)
                    o = bank(6 + n % 2)[:, m * HEAD:(m + 1) * HEAD]
                for k in range(nj):
                    ins = pe.matmul(o, probsT[:, q % 4, k * P:(k + 1) * P], v[:, j + k, cols],
                                    start=(j + k == 0), stop=(j + k == i))
                ins.then_inc(pv_done, 1)

            def attend(ph):
                scores(ph, 0)
                for s in range(STEPS):
                    if s + 1 < STEPS:
                        scores(ph, s + 1)
                    qs = quads[ph, s]
                    if ph == 1:
                        pe.wait_ge(exp_done, (STEPS + s) * 2 + 2)
                    turn(ph, s, qs[0])
                    for k, quad in enumerate(qs):
                        if k + 1 < len(qs):
                            turn(ph, s, qs[k + 1])
                        weigh(ph, s, quad)

            pe.wait_ge(bank_moved, before[B_GROUPS[0]])
            attend(0)
            pe.wait_ge(o_moved, STEPS)
            for g in B_GROUPS:
                project(g)
            pe.wait_ge(bank_moved, before[9])
            attend(1)

            def turn_mix(t):
                for half in range(2):
                    n = 2 * t + half
                    if t >= 2:
                        pe.wait_ge(mixT_lo, n - 3)
                    src = mixA if half == 0 else mixB
                    for c in range(4):
                        ins = pe.transpose(bank(n % 4)[:, c * P:(c + 1) * P], src[:, t, c * P:(c + 1) * P],
                                           ident[:, :])
                    ins.then_inc(mixT_ready, 1)

            pe.wait_ge(mixA_done, STEPS)
            pe.wait_ge(o_moved, 2 * STEPS)
            turn_mix(0)
            pe.wait_ge(w_lo_made, CHUNKS + 2 * DB)
            for t in range(TILES):
                if t + 1 < TILES:
                    turn_mix(t + 1)
                pe.wait_ge(mixT_lo, 2 * t + 2)
                if t >= 2:
                    pe.wait_ge(y_summed, t - 1)
                for half in range(2):
                    cols = slice(half * HALF, (half + 1) * HALF)
                    o = bank(4 + 2 * (t % 2) + half)
                    for e in range(DB):
                        for k, (a, w) in enumerate(((mx_hi, big_hi), (mx_hi, big_lo), (mx_lo, big_hi))):
                            ins = pe.matmul(o, a[:, t % 2, e, :], w[:, e, cols],
                                            start=(e == 0 and k == 0), stop=(e == DB - 1 and k == 2))
                ins.then_inc(y_ready, 1)

        @block.vector
        def _(dve):
            own = [0]

            def link(ins):
                own[0] += 1
                ins.then_inc(dve_own, 1)
                dve.wait_ge(dve_own, own[0])

            def inverse_root(root, var, done, a, b):
                link(dve.reciprocal(root, root))
                link(dve.tensor_tensor(a, root, root, ALU.mult))
                link(dve.tensor_tensor(a, a, var, ALU.mult))
                link(dve.tensor_scalar(a, a, -0.5, 1.5, ALU.mult, ALU.add))
                ins = dve.tensor_tensor(root, root, a, ALU.mult)
                if done is None:
                    link(ins)
                else:
                    ins.then_inc(done, 1)

            nh = A_HEADS + B_HEADS
            dve.memset(tableb[:, :, :], 1.0).then_inc(dve_own, 1)
            own[0] += 1
            dve.wait_ge(dve_own, own[0])
            dve.wait_ge(table_loaded, 32)
            for h in range(nh):
                ins = dve.tensor_scalar(tableb[:, h, :], tableb[:, h, :], table[:, h:h + 1], None, ALU.mult)
            ins.then_inc(tableb_made, 1)
            for h in range(nh):
                dve.wait_ge(band_ready, h + 1)
                dve.tensor_copy(band[:, h, :], bank(h % 8)[:, 0:RELS]).then_inc(band_out, 1)

            for t in range(TILES):
                dve.wait_ge(x_squared, t + 1)
                dve.tensor_scalar(varx[:, t:t + 1], ssx[:, t:t + 1], 1.0 / D_MODEL, EPS, ALU.mult, ALU.add
                                  ).then_inc(x_var, 1)
                dve.wait_ge(x_root, t + 1)
                inverse_root(rstd[:, t:t + 1], varx[:, t:t + 1], None, t_a, t_b)
                dve.tensor_scalar(xs[:, t, :], xs[:, t, :], rstd[:, t:t + 1], None, ALU.mult
                                  ).then_inc(x_scaled, 1)
            for n in range(2 * DB):
                half, d = divmod(n, DB)
                cols = slice(half * HALF, (half + 1) * HALF)
                dve.wait_ge(hT_hi, n + 1)
                dve.scalar_tensor_tensor(out=big_lo[:, d, cols], in0=bank(d), scalar=nw[:, d:d + 1],
                                         in1=big_hi[:, d, cols].bitcast(f32), op0=ALU.mult,
                                         op1=ALU.subtract).then_inc(hT_lo, 1)
            dve.wait_ge(consts_loaded, 16 * 6)
            for m in range(2):
                link(dve.tensor_tensor(lam4[:, 2 * m, :], lam4[:, 2 * m, :], lam4[:, 2 * m + 1, :], ALU.mult))
                ins = dve.reduce_sum(lam_s[:, m:m + 1], lam4[:, 2 * m, :], AX.X)
                link(ins)
            dve.tensor_copy(t_a, t_b if False else lam_s[:, 0:1]).then_inc(lam_sums, 1)
            dve.wait_ge(lam_exp, 1)
            link(dve.tensor_tensor(neglam, lam_e[:, 1:2], lam_e[:, 0:1], ALU.subtract))
            link(dve.tensor_scalar(neglam, neglam, -LAMBDA_INIT, None, ALU.add))
            dve.wait_ge(bias_loaded, 16 * nh)
            link(dve.memset(bias[0:CHUNK, :, BAND - CHUNK:BAND], MASKED))

            dve.wait_ge(iw_ready, 1)
            dve.tensor_copy(iw[:, :], psum[:, 3 * 2 * HALF:3 * 2 * HALF + TILES * IDX_HEADS]
                            ).then_inc(iw_moved, 1)
            dve.wait_ge(iw_moved, 1)
            n = 0
            for i in range(SEL0, TILES):
                sc = score[:, score_off[i]:score_off[i] + P * (i + 1)]
                for h in range(IDX_HEADS):
                    dve.wait_ge(idx_relu, n + 1)
                    r = relu[:, n % 2, 0:P * (i + 1)]
                    wcol = iw[:, i * IDX_HEADS + h:i * IDX_HEADS + h + 1]
                    if h == 0:
                        ins = dve.tensor_scalar(sc, r, wcol, None, ALU.mult)
                    else:
                        dve.wait_ge(idx_added, n)
                        ins = dve.scalar_tensor_tensor(out=sc, in0=r, scalar=wcol, in1=sc, op0=ALU.mult,
                                                       op1=ALU.add)
                    ins.then_inc(idx_added, 1)
                    n += 1
                dve.wait_ge(idx_added, n)
                link(dve.memset(score[0:CHUNK, score_off[i] + P * (i + 1) - CHUNK:
                                      score_off[i] + P * (i + 1)], UNSEEN))

            def select(rounds):
                for _ in range(rounds):
                    for i in range(SEL0, TILES):
                        sc = score[:, score_off[i]:score_off[i] + P * (i + 1)]
                        ins = dve.max(top8[:, i - SEL0, :], sc)
                        if i == TILES - 1:
                            link(ins)
                    for i in range(SEL0, TILES):
                        sc = score[:, score_off[i]:score_off[i] + P * (i + 1)]
                        ins = dve.match_replace(sc, top8[:, i - SEL0, :], sc, TAKEN)
                        if i == TILES - 1:
                            link(ins)

            def soften(ph, s):
                b, i = divmod(s, TILES)
                length = P * (i + 1)
                w = min(BAND, length)
                for m in range(2):
                    u = (ph * STEPS + s) * 2 + m
                    h = b if ph == 0 else A_HEADS + 2 * b + m
                    dve.wait_ge(s_ready, u + 1)
                    o = pair(m)[:, length - w:length]
                    link(dve.tensor_tensor(o, o, bias[:, h, BAND - w:BAND], ALU.add))
                    dve.tensor_reduce(negmax[:, u % 4:u % 4 + 1], pair(m)[:, 0:length], AX.X, ALU.max,
                                      negate=True).then_inc(max_ready, 1)

            def combine(s):
                i = s % TILES
                u = 2 * s
                c = u % 8
                dve.wait_ge(exp_done, u + 2)
                link(dve.reciprocal(rinv[:, c:c + 2], rsum[:, c:c + 2]))
                link(dve.scalar_tensor_tensor(out=comb_c[:, 0:1], in0=rsum[:, c:c + 1], scalar=neglam,
                                              in1=rinv[:, c + 1:c + 2], op0=ALU.mult, op1=ALU.mult))
                p1, p2 = (probs[:, (u + m) % 4, 0:P * (i + 1)] for m in range(2))
                dve.scalar_tensor_tensor(out=p1, in0=p2, scalar=comb_c[:, 0:1], in1=p1, op0=ALU.mult,
                                         op1=ALU.add).then_inc(combined, 1)

            def finishA(s):
                dve.wait_ge(pv_done, quads_through(0, s))
                if s >= 4:
                    dve.wait_ge(o_gated, s - 3)
                    dve.wait_ge(o_squared, s - 3)
                dve.tensor_scalar(o_tmp[:, s % 4, :], bank(6 + s % 2)[:, 0:P],
                                  rinv[:, (2 * s) % 8:(2 * s) % 8 + 1], None, ALU.mult
                                  ).then_inc(o_moved, 1)

            ROUNDS = TOPK // 8
            FIRST = ROUNDS // 2
            select(FIRST)
            soften(0, 0)
            for s in range(STEPS):
                combine(s)
                if s + 1 < STEPS:
                    soften(0, s + 1)
                if s >= 1:
                    finishA(s - 1)
            finishA(STEPS - 1)
            dve.wait_ge(o_squared, STEPS)
            link(dve.tensor_scalar(ssA, ssA, 1.0 / P, EPS, ALU.mult, ALU.add))
            dve.tensor_copy(t_a, ssA[:, 0:1]).then_inc(varA, 1)
            dve.wait_ge(rootA, 1)
            inverse_root(rA, ssA, rstdA, lam4[:, 0, 0:STEPS], None)
            select(ROUNDS - FIRST)
            for i in range(SEL0, TILES):
                o = slice(score_off[i], score_off[i] + P * (i + 1))
                dve.tensor_scalar(mask[:, o], score[:, o], TAKEN, MASKED, ALU.not_equal, ALU.mult
                                  ).then_inc(mask_made, 1)

            def turned(s):
                for q, m, j, nj in quads[1, s]:
                    dve.wait_ge(t_ready, q + 1)
                    dve.wait_ge(pv_done, q - 3)
                    dve.tensor_copy(probsT[:, q % 4, 0:nj * P], bank(4 + q % 2)[:, 0:nj * P]
                                    ).then_inc(t_moved, 1)

            def finishB(s):
                b, i = divmod(s, TILES)
                n = STEPS + s
                c = (2 * n) % 8
                link(dve.reciprocal(rinv[:, c:c + 2], rsum[:, c:c + 2]))
                dve.wait_ge(pv_done, quads_through(1, s))
                for m in range(2):
                    g = mixB[:, i, b * P + m * HEAD:b * P + (m + 1) * HEAD]
                    ins = dve.scalar_tensor_tensor(out=g, in0=bank(6 + n % 2)[:, m * HEAD:(m + 1) * HEAD],
                                                   scalar=rinv[:, c + m:c + m + 1], in1=g, op0=ALU.mult,
                                                   op1=ALU.mult)
                ins.then_inc(o_moved, 1)

            soften(1, 0)
            dve.wait_ge(bank_moved, before[9])
            for s in range(STEPS):
                if s + 1 < STEPS:
                    soften(1, s + 1)
                turned(s)
                dve.wait_ge(exp_done, (STEPS + s) * 2 + 2)
                finishB(s)

            for t in range(TILES + 1):
                if t < TILES:
                    for half in range(2):
                        n = 2 * t + half
                        dve.wait_ge(mixT_hi, n + 1)
                        blk = slice(half * 4, half * 4 + 4)
                        dve.tensor_tensor(mx_lo[:, t % 2, blk, :],
                                          bank(n % 4)[:, :].rearrange("p (c q) -> p c q", q=P),
                                          mx_hi[:, t % 2, blk, :].bitcast(f32), ALU.subtract
                                          ).then_inc(mixT_lo, 1)
                if t >= 1:
                    k = t - 1
                    dve.wait_ge(y_ready, k + 1)
                    dve.wait_ge(xres_loaded[k % 2], 16 * (k // 2 + 1))
                    if k >= 2:
                        dve.wait_ge(y_squared, k - 1)
                        dve.wait_ge(y_scaled, k - 1)
                    dve.tensor_tensor(y[:, k % 2, :], pair(2 + k % 2), xres[:, k % 2, :], ALU.add
                                      ).then_inc(y_summed, 1)
                    dve.wait_ge(y_squared, k + 1)
                    dve.tensor_scalar(varx[:, k:k + 1], ssx[:, k:k + 1], 1.0 / D_MODEL, EPS, ALU.mult,
                                      ALU.add).then_inc(y_var, 1)
                    dve.wait_ge(y_root, k + 1)
                    inverse_root(rstd[:, k:k + 1], varx[:, k:k + 1], None, t_a, t_b)
                    dve.wait_ge(fw_loaded, 16)
                    if k >= 2:
                        dve.wait_ge(stored[k % 2], 16 * (k // 2))
                    dve.scalar_tensor_tensor(out=y_out[:, k % 2, :], in0=y[:, k % 2, :],
                                             scalar=rstd[:, k:k + 1], in1=fw[:, :], op0=ALU.mult,
                                             op1=ALU.mult).then_inc(y_scaled, 1)


INPUTS = ["x", "norm_w", "w_in", "w_out", "lambda_q1", "lambda_k1", "lambda_q2", "lambda_k2",
          "subln_w", "rel_bias", "final_norm_w"]


def kernel(**inputs):
    import concourse.bacc as bacc
    from concourse.bass_utils import run_bass_kernel_spmd

    nc = bacc.Bacc("TRN2", target_bir_lowering=False, num_devices=1)
    f32 = mybir.dt.float32
    arrays, args = {}, []
    for name in INPUTS:
        arrays[f"in_{name}"] = np.ascontiguousarray(inputs[name])
    arrays["in_selector"] = bucket_selector()
    for name, a in arrays.items():
        args.append(nc.dram_tensor(name, a.shape, f32, kind="ExternalInput").ap())
    args.append(nc.dram_tensor("out_y", (1, SEQ, D_MODEL), f32, kind="ExternalOutput").ap())
    build(nc, *args)
    r = run_bass_kernel_spmd(nc, [arrays], core_ids=[0])
    return r.results[0]["out_y"]
```

```python
import math

import concourse.bass as bass
import numpy as np
from concourse import mybir

SEQ, D_MODEL = 1024, 1024
P = 128
CHUNK = 64
TILES = SEQ // P
DB = D_MODEL // P
WIDTH = 512
HALF = 512
HEAD = 64
BLOCKS = WIDTH // P
A_HEADS, B_HEADS = 4, 8
IDX_HEADS = 4
IDX_COL = 8 * WIDTH
IDX_COLS = IDX_HEADS * HEAD + HEAD + IDX_HEADS
TOPK = 256
SEL0 = TOPK // P
BUCKETS, MAX_DISTANCE = 32, 128
EPS = 1e-6
LAMBDA_INIT = 0.8 - 0.6 * math.exp(0.0)
QK_SCALE = HEAD ** -0.5
IDX_SCALE = IDX_HEADS ** -0.5 * HEAD ** -0.5
MASKED = 1e30
UNSEEN = -3e38
UNSEEN_MIN = 3e38
TAKEN = -2e38
REL0 = -(2 * P - 1)
RELS = 3 * P
BAND = 2 * P
SW = 3


def bucket_selector():
    rel = REL0 + np.arange(RELS)
    nb = BUCKETS // 2
    exact = nb // 2
    n = np.abs(rel)
    nf = np.maximum(n, 1).astype(np.float32)
    large = exact + (np.log(nf / np.float32(exact)) / np.float32(math.log(MAX_DISTANCE / exact))
                     * np.float32(nb - exact)).astype(np.int32)
    large = np.minimum(large, nb - 1)
    bucket = np.where(rel > 0, nb, 0) + np.where(n < exact, n, large)
    hot = np.zeros((BUCKETS, RELS), np.float32)
    hot[bucket, np.arange(RELS)] = 1.0
    hot[nb - 1, :] -= 1.0
    return -hot


def build(nc, x, norm_w, w_in, w_out, lambda_q1, lambda_k1, lambda_q2, lambda_k2, subln_w,
          rel_bias, final_norm_w, selector, out):
    f32, f32r, bf16 = mybir.dt.float32, mybir.dt.float32r, mybir.dt.bfloat16
    ALU, ACT, AX = mybir.AluOpType, mybir.ActivationFunctionType, mybir.AxisListType

    top = [(nc.sbuf_base + 63) // 64 * 64]

    def place(name, shape, dt, at=None):
        size = int(np.prod(shape[1:])) * (2 if dt == bf16 else 4)
        if at is None:
            at = top[0]
            top[0] += (size + 31) // 32 * 32
        return nc.alloc_sbuf_tensor_at(name, shape, dt, offset=at), at

    big_hi, _ = place("big_hi", [P, DB, SEQ], f32r)
    big_lo, _ = place("big_lo", [P, DB, SEQ], f32r)
    qT, qT_at = place("qT", [P, BLOCKS, SEQ], f32)
    kT, kT_at = place("kT", [P, BLOCKS, SEQ], f32)
    v, v_at = place("v", [P, TILES, WIDTH], f32)
    mixA, _ = place("mixA", [P, TILES, WIDTH], f32)
    score_at = top[0]
    score_off = {}
    total = 0
    for i in range(SEL0, TILES):
        score_off[i] = total
        total += P * (i + 1)
    score, _ = place("score", [P, max(total, TILES * WIDTH)], f32)
    mixB, _ = place("mixB", [P, TILES, WIDTH], f32, at=score_at)
    mask, mask_at = place("mask", [P, total], bf16)
    bias, _ = place("bias", [P, A_HEADS + B_HEADS, BAND], f32)
    w_raw, _ = place("w_raw", [P, SW, WIDTH], f32)
    probs, probs_at = place("probs", [P, 4, SEQ], f32)
    w_hi, w_hi_at = place("w_hi", [P, SW, WIDTH], f32r)
    w_lo, _ = place("w_lo", [P, SW, WIDTH], f32r)
    ident, _ = place("ident", [P, P], f32)
    identb, _ = place("identb", [P, P], bf16)
    subln, _ = place("subln", [P, P], f32)
    o_tmp, _ = place("o_tmp", [P, 4, P], f32)
    sq_junk, _ = place("sq_junk", [P, P], bf16)
    nw, _ = place("nw", [P, DB], f32)
    probs_x, _ = place("probs_x", [P, 1, SEQ], f32)
    iw, _ = place("iw", [P, TILES * IDX_HEADS], f32)
    small, _ = place("small", [P, 128], f32)
    top8, _ = place("top8", [P, TILES - SEL0, 8], f32)
    assert top[0] <= nc.sbuf_usable_end, (top[0], nc.sbuf_usable_end)
    probsT = [place("probsT_A", [P, 4, HALF], f32, at=mask_at)[0],
              place("probsT_B", [P, 4, HALF], f32, at=w_hi_at)[0]]
    lam4, _ = place("lam4", [P, 4, HEAD], f32, at=mask_at + 4096)
    xs, _ = place("xs", [P, TILES, D_MODEL], f32, at=qT_at)
    x_junk, _ = place("x_junk", [P, D_MODEL], bf16, at=probs_at + 12 * 1024)
    iqT, _ = place("iqT", [P, 2, SEQ], f32, at=v_at)
    ikT, _ = place("ikT", [P, SEQ], f32, at=v_at + 8192)
    iwT, _ = place("iwT", [IDX_HEADS, SEQ], f32, at=mask_at)
    relu, _ = place("relu", [P, 2, SEQ], f32, at=probs_at)
    table, _ = place("table", [BUCKETS, A_HEADS + B_HEADS], f32, at=probs_at)
    nw8, _ = place("nw8", [DB, P], f32, at=probs_at + 8192)
    sel, _ = place("sel", [BUCKETS, RELS], f32, at=probs_at + 64)
    tableb, _ = place("tableb", [BUCKETS, A_HEADS + B_HEADS, P], f32, at=probs_at + 64 + 4 * RELS)
    band, _ = place("band", [P, A_HEADS + B_HEADS, RELS], f32, at=v_at + 12288)
    mx_hi, _ = place("mx_hi", [P, 2, DB, P], f32r, at=qT_at)
    mx_lo, _ = place("mx_lo", [P, 2, DB, P], f32r, at=qT_at + 8192)
    xres, _ = place("xres", [P, 2, D_MODEL], f32, at=kT_at)
    fw, _ = place("fw", [P, D_MODEL], f32, at=kT_at + 8192)
    y, _ = place("y", [P, 2, D_MODEL], f32, at=v_at)
    y_out, _ = place("y_out", [P, 2, D_MODEL], f32, at=v_at + 8192)
    y_junk, _ = place("y_junk", [P, D_MODEL], bf16, at=kT_at + 12288)

    rstd = small[:, 0:8]
    t_a = small[:, 8:10]
    warm = small[:, 126:127]
    ssx = small[:, 10:18]
    neglam = small[:, 18:19]
    lam_e = small[:, 20:22]
    negmax = small[:, 24:28]
    farmin = small[:, 80:84]
    rsum = small[:, 28:36]
    rinv = small[:, 36:44]
    comb_c = small[:, 44:46]
    ssA = small[:, 48:80]
    rA = small[:, 84:116]
    lam_s = small[:, 116:118]
    varx = small[:, 118:126]

    from contextlib import ExitStack
    ctx = ExitStack()
    with ctx:
        def sem(name):
            return ctx.enter_context(nc.semaphore(name))

        psum = ctx.enter_context(nc.psum_tensor("psum", [P, 8 * HALF], f32))
        scratch = nc.dram_tensor("bias_scratch", [P * (A_HEADS + B_HEADS) * RELS], f32, kind="Internal")

        def bank(n):
            return psum[:, n * HALF:(n + 1) * HALF]

        def pair(n):
            return psum[:, n * 2 * HALF:(n + 1) * 2 * HALF]

        x_loaded = [sem(f"x_loaded{t}") for t in range(TILES)]
        consts_loaded = sem("consts_loaded")
        table_loaded = sem("table_loaded")
        nw_loaded = sem("nw_loaded")
        nw_turned = sem("nw_turned")
        nw_moved = sem("nw_moved")
        band_stored = sem("band_stored")
        bias_loaded = sem("bias_loaded")
        w_loaded = [sem(f"w_loaded{r}") for r in range(SW)]
        xres_loaded = [sem(f"xres_loaded{r}") for r in range(2)]
        fw_loaded = sem("fw_loaded")
        stored = [sem(f"stored{r}") for r in range(2)]
        consts_made = sem("consts_made")
        x_squared = sem("x_squared")
        x_var = sem("x_var")
        x_root = sem("x_root")
        x_rstd = sem("x_rstd")
        x_scaled = [sem("x_scaled_dve"), sem("x_scaled_pool")]
        warm_made = sem("warm_made")
        hT_ready = sem("hT_ready")
        hT_hi = sem("hT_hi")
        hT_lo = sem("hT_lo")
        lam_sums = sem("lam_sums")
        lam_exp = sem("lam_exp")
        lam_ready = sem("lam_ready")
        tableb_made = sem("tableb_made")
        band_ready = sem("band_ready")
        band_out = sem("band_out")
        w_hi_made = sem("w_hi_made")
        w_lo_made = sem("w_lo_made")
        chunk_used = sem("chunk_used")
        bank_ready = sem("bank_ready")
        bank_moved = sem("bank_moved")
        ik_moved = sem("ik_moved")
        iw_ready = sem("iw_ready")
        iw_moved = sem("iw_moved")
        idx_ready = sem("idx_ready")
        idx_relu = sem("idx_relu")
        idx_added = sem("idx_added")
        mask_made = sem("mask_made")
        s_ready = sem("s_ready")
        max_ready = sem("max_ready")
        exp_done = sem("exp_done")
        combined = sem("combined")
        t_ready = sem("t_ready")
        t_moved = [sem("t_moved_act"), sem("t_moved_dve")]
        pv_done = sem("pv_done")
        o_moved = sem("o_moved")
        o_squared = sem("o_squared")
        o_gated = sem("o_gated")
        gateA_scaled = sem("gateA_scaled")
        rootA = sem("rootA")
        varA = sem("varA")
        rstdA = sem("rstdA")
        mixA_done = sem("mixA_done")
        wout_hi = sem("wout_hi")
        wout_lo = sem("wout_lo")
        mixT_ready = sem("mixT_ready")
        mixT_hi = sem("mixT_hi")
        mixT_lo = sem("mixT_lo")
        y_ready = sem("y_ready")
        y_summed = sem("y_summed")
        y_squared = sem("y_squared")
        y_var = sem("y_var")
        y_root = sem("y_root")
        y_scaled = sem("y_scaled")
        dve_own = sem("dve_own")
        pool_own = sem("pool_own")

        GROUPS = [(IDX_COL, IDX_COLS, "T")]
        for g in range(2):
            for n in range(4):
                GROUPS.append(((4 * g + n) * WIDTH, WIDTH, "T" if n < 2 else "N"))
        banks = [6] + [8] * 8
        before = [sum(banks[:g]) for g in range(10)]
        moved = [0] + [n - 1 for n in before[1:]]
        A_GROUPS, B_GROUPS = range(1, 5), range(5, 9)
        CHUNKS = len(GROUPS) * DB

        ORDER = ([7, 6, 4, 2, 0, 1, 3, 5], [5, 3, 4, 2, 0, 1, 6, 7])
        STEPS = BLOCKS * TILES

        def place_of(ph, s):
            return s // TILES, ORDER[ph][s % TILES]

        quads = {}
        n = 0
        for ph in range(2):
            for s in range(STEPS):
                nb = place_of(ph, s)[1] + 1
                quads[ph, s] = []
                for m in ([0] if ph == 0 else [0, 1]):
                    for j in range(0, nb, 4):
                        quads[ph, s].append((n, m, j, min(4, nb - j)))
                        n += 1

        def probs_of(ph, s, m):
            if ph == 1:
                return probs[:, (2 * s + m) % 4, :]
            if m == 0:
                return probs[:, s % 3, :]
            return probs[:, 3, :] if s % 2 == 0 else probs_x[:, 0, :]

        S_BANKS, O_BANK, T_BANK = 5, 5, 6
        score_bank, bank_free = {}, {}
        last = [-1] * S_BANKS
        for u in range(4 * STEPS):
            need = 1 if place_of(u // (2 * STEPS), u // 2 % STEPS)[1] < HALF // P else 2
            first = min(range(S_BANKS - need + 1), key=lambda k: (max(last[k:k + need]), k))
            score_bank[u], bank_free[u] = first, max(last[first:first + need])
            last[first:first + need] = [u] * need

        def score_of(u, c0, c1):
            return psum[:, score_bank[u] * HALF + c0:score_bank[u] * HALF + c1]

        quads_A = quads[0, STEPS - 1][-1][0] + 1
        mover, moves = {}, {}
        for q in range(n):
            mover[q] = q % 2 if q >= quads_A else 0
            moves[q] = sum(mover[k] == mover[q] for k in range(q + 1))

        def wait_moved(q):
            nc.tensor.wait_ge(t_moved[mover[q]], moves[q])

        def quads_through(ph, s):
            return quads[ph, s][-1][0] + 1

        def column_block(g, t):
            c, half = divmod(t, 2)
            return ((2, 0, 1)[c] if g == 0 else c), half

        def wait_chunk_used(eng, n):
            g, d = divmod(n, DB)
            if d == DB - 1:
                eng.wait_ge(bank_ready, before[g + 1])
            else:
                eng.wait_ge(chunk_used, g * (DB - 1) + d + 1)

        block = ctx.enter_context(nc.Block())

        @block.sync
        def _(sp):
            for t in range(TILES):
                sp.dma_start(xs[:, t, :], x[0, t * P:(t + 1) * P, :]).then_inc(x_loaded[t], 16)
                if t == 0:
                    sp.dma_start(nw8[:, :], norm_w.rearrange("o (c p) -> (o c) p", p=P)).then_inc(nw_loaded, 16)
                    sp.dma_start(table[:, :], rel_bias).then_inc(table_loaded, 16)
                    sp.dma_start(sel[:, :], selector).then_inc(table_loaded, 16)

            def load_chunk(n):
                if n >= SW:
                    sp.wait_ge(w_lo_made, n - SW + 1)
                if n < CHUNKS:
                    c0, cols, _ = GROUPS[n // DB]
                    d = n % DB
                    src = w_in[0, d * P:(d + 1) * P, c0:c0 + cols]
                else:
                    d, half = divmod(n - CHUNKS, 2)
                    cols = WIDTH
                    src = w_out[0, d * P:(d + 1) * P, half * WIDTH:(half + 1) * WIDTH]
                sp.dma_start(w_raw[:, n % SW, 0:cols], src).then_inc(w_loaded[n % SW], 16)

            for n in range(DB + SW):
                load_chunk(n)
                if n == 0:
                    sp.dma_start(subln[:, :], subln_w.to_broadcast([P, P])).then_inc(consts_loaded, 16)
                    for k, row in enumerate((lambda_q1, lambda_k1, lambda_q2, lambda_k2)):
                        sp.dma_start(lam4[:, k, :], row.to_broadcast([P, HEAD])).then_inc(consts_loaded, 16)
            nh = A_HEADS + B_HEADS
            sp.wait_ge(band_out, nh)
            sp.dma_start(bass.AP(scratch, 0, [[nh * RELS, P], [1, nh * RELS]]),
                         band[:, :, :].rearrange("p h r -> p (h r)")).then_inc(band_stored, 16)
            sp.wait_ge(band_stored, 16)
            for h in range(nh):
                sp.dma_start(bias[:, h, :],
                             bass.AP(scratch, h * RELS + P - 1, [[nh * RELS - 1, P], [1, BAND]])
                             ).then_inc(bias_loaded, 16)
            for n in range(DB + SW, CHUNKS + 2 * DB):
                load_chunk(n)
            sp.wait_ge(pv_done, quads_through(1, STEPS - 1))
            sp.dma_start(fw[:, :], final_norm_w.rearrange("(o n) -> o n", o=1).to_broadcast([P, D_MODEL])
                         ).then_inc(fw_loaded, 16)
            for t in range(TILES + 1):
                if t < TILES:
                    if t >= 2:
                        sp.wait_ge(y_summed, t - 1)
                    sp.dma_start(xres[:, t % 2, :], x[0, t * P:(t + 1) * P, :]
                                 ).then_inc(xres_loaded[t % 2], 16)
                if t >= 1:
                    sp.wait_ge(y_scaled, t)
                    sp.dma_start(out[0, (t - 1) * P:t * P, :], y_out[:, (t - 1) % 2, :]
                                 ).then_inc(stored[(t - 1) % 2], 16)
            sp.wait_ge(stored[0], 16 * (TILES // 2))
            sp.wait_ge(stored[1], 16 * (TILES // 2))

        @block.gpsimd
        def _(pool):
            own = [0]

            def link(ins):
                own[0] += 1
                ins.then_inc(pool_own, 1)
                pool.wait_ge(pool_own, own[0])

            for tile in (ident, identb):
                link(pool.memset(tile[:, :], 0.0))
                pool.affine_select(out=tile[:, :], in_=tile[:, :], compare_op=ALU.not_equal, fill=1.0,
                                   base=0, pattern=[[-1, P]], channel_multiplier=1
                                   ).then_inc(consts_made, 1)
            link(pool.memset(tableb[:, :, :], 1.0))
            for t in range(1, TILES, 2):
                pool.wait_ge(x_rstd, t // 2 + 1)
                pool.tensor_scalar(xs[:, t, :], xs[:, t, :], rstd[:, t:t + 1], 0.0, ALU.mult, ALU.add
                                   ).then_inc(x_scaled[1], 1)
                if t == 3:
                    pool.wait_ge(table_loaded, 32)
                    for h in range(A_HEADS + B_HEADS):
                        ins = pool.tensor_scalar(tableb[:, h, :], tableb[:, h, :], table[:, h:h + 1], 0.0,
                                                 ALU.mult, ALU.add)
                    ins.then_inc(tableb_made, 1)

            def low(n):
                cols = GROUPS[n // DB][1]
                pool.wait_ge(w_hi_made, n + 1)
                r = n % SW
                pool.tensor_tensor(w_lo[:, r, 0:cols], w_raw[:, r, 0:cols],
                                   w_hi[:, r, 0:cols].bitcast(f32), ALU.subtract
                                   ).then_inc(w_lo_made, 1)

            for n in range(A_GROUPS[-1] * DB + DB):
                low(n)
            pool.wait_ge(consts_loaded, 16 * 5)
            link(pool.tensor_scalar(subln[:, :], subln[:, :], 1.0 - LAMBDA_INIT, 0.0, ALU.mult, ALU.add))
            for t in range(TILES):
                pool.wait_ge(bank_moved, moved[A_GROUPS[-1]] + t + 1)
                for b in range(BLOCKS):
                    g = mixA[:, t, b * P:(b + 1) * P]
                    ins = pool.tensor_tensor(g, g, subln[:, :], ALU.mult)
                ins.then_inc(gateA_scaled, 1)
            pool.wait_ge(gateA_scaled, TILES)
            for s in range(STEPS):
                b, i = place_of(0, s)
                g = mixA[:, i, b * P:(b + 1) * P]
                pool.wait_ge(o_moved, s + 1)
                pool.tensor_tensor(g, g, o_tmp[:, s % 4, :], ALU.mult).then_inc(o_gated, 1)
                if s in (9, 13, 17):
                    low(B_GROUPS[0] * DB + s // 4 - 2)
            for n in range(B_GROUPS[0] * DB + SW, CHUNKS):
                low(n)
                if n == B_GROUPS[0] * DB + DB:
                    pool.wait_ge(rstdA, 1)
                    pool.wait_ge(o_gated, STEPS)
                    for s in range(STEPS):
                        b, i = place_of(0, s)
                        g = mixA[:, i, b * P:(b + 1) * P]
                        pool.tensor_scalar(g, g, rA[:, s:s + 1], 0.0, ALU.mult, ALU.add
                                           ).then_inc(mixA_done, 1)
            wait_chunk_used(pool, CHUNKS - 1)
            for n in range(CHUNKS, CHUNKS + 2 * DB):
                d, half = divmod(n - CHUNKS, 2)
                dst = slice(half * WIDTH, (half + 1) * WIDTH)
                pool.wait_ge(w_loaded[n % SW], 16 * (n // SW + 1))
                pool.tensor_scalar(big_hi[:, d, dst], w_raw[:, n % SW, :], 1.0, 0.0, ALU.mult, ALU.add
                                   ).then_inc(wout_hi, 1)
                pool.wait_ge(wout_hi, n - CHUNKS + 1)
                pool.tensor_tensor(big_lo[:, d, dst], w_raw[:, n % SW, :],
                                   big_hi[:, d, dst].bitcast(f32), ALU.subtract).then_inc(w_lo_made, 1)

        @block.scalar
        def _(act):
            act.wait_ge(warm_made, 1)
            act.activation(warm, warm, ACT.Sqrt)
            for t in range(TILES + 1):
                if t < TILES:
                    act.wait_ge(x_loaded[t], 16)
                    if t >= 1:
                        act.wait_ge(x_squared, t)
                    act.activation(x_junk[:, :], xs[:, t, :], ACT.Square, accum_out=ssx[:, t:t + 1]
                                   ).then_inc(x_squared, 1)
                if t >= 2 and t % 2 == 0:
                    act.wait_ge(x_var, t // 2)
                    act.activation(rstd[:, t - 2:t], varx[:, t - 2:t], ACT.Sqrt).then_inc(x_root, 1)

            def high(n):
                cols = GROUPS[n // DB][1]
                act.wait_ge(w_loaded[n % SW], 16 * (n // SW + 1))
                if n >= SW:
                    wait_chunk_used(act, n - SW)
                act.activation(w_hi[:, n % SW, 0:cols], w_raw[:, n % SW, 0:cols], ACT.Copy
                               ).then_inc(w_hi_made, 1)

            act.wait_ge(nw_moved, 1)
            for n in range(2 * DB):
                half, d = divmod(n, DB)
                act.wait_ge(hT_ready, n + 1)
                act.activation(big_hi[:, d, half * HALF:(half + 1) * HALF], bank(d), ACT.Copy,
                               scale=nw[:, d:d + 1]).then_inc(hT_hi, 1)
                if n in (DB - 1, DB, DB + 2):
                    high({DB - 1: 0, DB: 1, DB + 2: 2}[n])

            def move(g):
                kind = GROUPS[g][2]
                for t in range(banks[g]):
                    if g == 0 and t == 1:
                        continue
                    act.wait_ge(bank_ready, before[g] + t + 1)
                    c, half = column_block(g, t)
                    cols = slice(half * HALF, (half + 1) * HALF)
                    if g == 0:
                        if c < 2:
                            ins = act.activation(iqT[:, c, cols], bank(t), ACT.Copy)
                        else:
                            act.activation(ikT[0:HEAD, cols], bank(t)[0:HEAD, :], ACT.Copy)
                            act.activation(ikT[HEAD:P, cols], bank(t)[0:HEAD, :], ACT.Copy)
                            ins = act.activation(iwT[:, cols], bank(t)[HEAD:HEAD + IDX_HEADS, :],
                                                 ACT.Copy, scale=IDX_SCALE)
                    elif kind == "T":
                        is_q = g in (A_GROUPS[0], B_GROUPS[0])
                        ins = act.activation((qT if is_q else kT)[:, c, cols], bank(t), ACT.Copy,
                                             scale=-QK_SCALE if is_q else 1.0)
                    elif g in (A_GROUPS[2], B_GROUPS[2]):
                        ins = act.activation(v[:, t, :], bank(t), ACT.Copy)
                    else:
                        if g == B_GROUPS[3] and t == 0:
                            act.wait_ge(mask_made, TILES - SEL0)
                        ins = act.activation((mixA if g == A_GROUPS[3] else mixB)[:, t, :], bank(t),
                                             ACT.Silu)
                    ins.then_inc(bank_moved, 1)

            def project(groups, last):
                for g in groups:
                    for d in range(DB):
                        if g * DB + d >= started[0]:
                            high(g * DB + d)
                        if d == 1 and g > groups[0]:
                            move(g - 1)
                    started[0] = max(started[0], (g + 1) * DB)
                if last:
                    move(groups[-1])

            started = [3]
            project([0], False)
            high(DB)
            high(DB + 1)
            started[0] = DB + 2
            move(0)
            n = 0
            for i in range(SEL0, TILES):
                for h in range(IDX_HEADS):
                    act.wait_ge(idx_ready, n + 1)
                    if n >= 2:
                        act.wait_ge(idx_added, n - 1)
                    act.activation(relu[:, n % 2, 0:P * (i + 1)], pair(n % 4)[:, 0:P * (i + 1)],
                                   ACT.Relu).then_inc(idx_relu, 1)
                    n += 1
            act.wait_ge(lam_sums, 2)
            act.activation(lam_e, lam_s, ACT.Exp).then_inc(lam_exp, 1)

            project(list(A_GROUPS), True)

            def exp(ph, s, m):
                length = P * (place_of(ph, s)[1] + 1)
                u = (ph * STEPS + s) * 2 + m
                act.wait_ge(max_ready, u + 1)
                if ph == 0 and m == 0 and s >= 3:
                    act.wait_ge(t_ready, quads_through(0, s - 3))
                if ph == 0 and m == 1 and s >= 2:
                    act.wait_ge(combined, s - 1)
                if ph == 1 and s >= 2:
                    act.wait_ge(t_ready, quads_through(1, s - 2))
                act.activation(probs_of(ph, s, m)[:, 0:length], score_of(u, 0, length), ACT.Exp,
                               bias=negmax[:, u % 4:u % 4 + 1], scale=-1.0,
                               accum_out=rsum[:, u % 8:u % 8 + 1]).then_inc(exp_done, 1)

            def turned(ph, quads):
                for q, m, j, nj in quads:
                    if mover[q] == 0:
                        act.wait_ge(t_ready, q + 1)
                        if q >= 4:
                            act.wait_ge(pv_done, q - 3)
                        act.activation(probsT[ph][:, q % 4, 0:nj * P], bank(T_BANK + q % 2)[:, 0:nj * P], ACT.Copy
                                       ).then_inc(t_moved[0], 1)

            def finish(s):
                if s >= 1:
                    act.wait_ge(o_squared, s)
                act.wait_ge(o_moved, s + 1)
                act.activation(sq_junk[:, :], o_tmp[:, s % 4, :], ACT.Square,
                               accum_out=ssA[:, s:s + 1]).then_inc(o_squared, 1)

            exp(0, 0, 0)
            exp(0, 0, 1)
            for s in range(STEPS + 2):
                qs = quads[0, s - 1] if 1 <= s <= STEPS else []
                turned(0, qs)
                if s + 1 < STEPS:
                    exp(0, s + 1, 0)
                    exp(0, s + 1, 1)
                if s >= 2:
                    finish(s - 2)
                if s in (8, 12, 16):
                    high(B_GROUPS[0] * DB + s // 4 - 2)
            started[0] = B_GROUPS[0] * DB + SW
            act.wait_ge(varA, 1)
            act.activation(rA, ssA, ACT.Sqrt).then_inc(rootA, 1)
            project(list(B_GROUPS), True)

            exp(1, 0, 0)
            exp(1, 0, 1)
            for s in range(STEPS):
                qs = quads[1, s]
                turned(1, qs[0:2])
                if s + 1 < STEPS:
                    exp(1, s + 1, 0)
                turned(1, qs[2:3])
                if s + 1 < STEPS:
                    exp(1, s + 1, 1)
                turned(1, qs[3:])

            for t in range(TILES + 1):
                if t < TILES:
                    for half in range(2):
                        n = 2 * t + half
                        act.wait_ge(mixT_ready, n + 1)
                        if t >= 2:
                            act.wait_ge(y_ready, t - 1)
                        act.activation(mx_hi[:, t % 2, half * 4:half * 4 + 4, :],
                                       bank(n % 4)[:, :].rearrange("p (c q) -> p c q", q=P), ACT.Copy
                                       ).then_inc(mixT_hi, 1)
                if t >= 1:
                    act.wait_ge(y_summed, t)
                    if t >= 2:
                        act.wait_ge(y_squared, t - 1)
                    act.activation(y_junk[:, :], y[:, (t - 1) % 2, :], ACT.Square,
                                   accum_out=ssx[:, t - 1:t]).then_inc(y_squared, 1)
                    act.wait_ge(y_var, t)
                    act.activation(rstd[:, t - 1:t], varx[:, t - 1:t], ACT.Sqrt).then_inc(y_root, 1)

        @block.tensor
        def _(pe):
            pe.wait_ge(consts_made, 2)
            pe.wait_ge(nw_loaded, 16)
            pe.transpose(bank(7)[:, 0:DB], nw8[:, :], ident[0:DB, 0:DB]).then_inc(nw_turned, 1)
            def turn_x(tt, d):
                ins = pe.transpose(bank(d)[:, tt % 4 * P:(tt % 4 + 1) * P],
                                   xs[:, tt, d * P:(d + 1) * P], ident[:, :])
                if tt % 4 == 3:
                    ins.then_inc(hT_ready, 1)

            for tt in range(4):
                pe.wait_ge(x_scaled[tt % 2], tt // 2 + 1)
                for d in range(DB):
                    if tt == 0 and d == DB - 1:
                        pe.wait_ge(nw_moved, 1)
                    turn_x(tt, d)
            for d in range(DB):
                pe.wait_ge(hT_lo, d + 1)
                for tt in range(4, TILES):
                    if d == 0:
                        pe.wait_ge(x_scaled[tt % 2], tt // 2 + 1)
                    turn_x(tt, d)

            def bias_row(h):
                pe.wait_ge(tableb_made, 1)
                pe.wait_ge(hT_lo, 2 * DB)
                if h >= 2:
                    pe.wait_ge(band_out, h - 1)
                pe.matmul(bank(6 + h % 2)[:, 0:RELS], tableb[:, h, :], sel[:, :], start=True, stop=True
                          ).then_inc(band_ready, 1)

            def project(g):
                c0, cols, kind = GROUPS[g]
                for d in range(DB):
                    n = g * DB + d
                    r = n % SW
                    pe.wait_ge(w_lo_made, n + 1)
                    if g == 0:
                        pe.wait_ge(hT_lo, DB + d + 1)
                    for t in range(banks[g]):
                        if d == 0 and g == A_GROUPS[0]:
                            pe.wait_ge(idx_relu, (TILES - SEL0) * IDX_HEADS - 3 + t // 2)
                        elif d == 0 and g == B_GROUPS[0]:
                            if t == O_BANK:
                                pe.wait_ge(o_moved, STEPS)
                            elif t >= T_BANK:
                                wait_moved(quads_A - 1)
                        elif d == 0 and g > 0:
                            pe.wait_ge(bank_moved, moved[g - 1] + t + 1)
                        if g == 0 and d == 0:
                            pe.wait_ge(hT_lo, DB + t + 1)
                        if kind == "T":
                            c, half = column_block(g, t)
                            m = min(P, cols - c * P)
                            ws = slice(c * P, c * P + m)
                            hs = slice(half * HALF, (half + 1) * HALF)
                            o = bank(t)[0:m, :]
                            passes = [(w_hi[:, r, ws], big_hi[:, d, hs]), (w_hi[:, r, ws], big_lo[:, d, hs]),
                                      (w_lo[:, r, ws], big_hi[:, d, hs])]
                        else:
                            hs = slice(t * P, (t + 1) * P)
                            o = bank(t)
                            passes = [(big_hi[:, d, hs], w_hi[:, r, :]), (big_hi[:, d, hs], w_lo[:, r, :]),
                                      (big_lo[:, d, hs], w_hi[:, r, :])]
                        for k, (a, b) in enumerate(passes):
                            ins = pe.matmul(o, a, b, start=(d == 0 and k == 0),
                                            stop=(d == DB - 1 and k == 2))
                        if d == DB - 1:
                            ins.then_inc(bank_ready, 1)
                    if d < DB - 1:
                        ins.then_inc(chunk_used, 1)
                    if g == 0 and 1 <= d <= 6:
                        bias_row(2 * d - 2)
                        bias_row(2 * d - 1)

            project(0)
            n = 0
            for i in range(SEL0, TILES):
                for h in range(IDX_HEADS):
                    if n == 0:
                        pe.wait_ge(bank_moved, 3)
                        pe.wait_ge(ik_moved, 1)
                    elif n == 2:
                        pe.wait_ge(bank_moved, moved[1])
                    elif n == 3:
                        pe.wait_ge(band_out, A_HEADS + B_HEADS)
                        for t in range(TILES):
                            ins = pe.transpose(bank(7)[:, 4 * t:4 * t + 4], iwT[:, t * P:(t + 1) * P],
                                               ident[0:IDX_HEADS, 0:IDX_HEADS])
                        ins.then_inc(iw_ready, 1)
                    elif n >= 4:
                        pe.wait_ge(idx_relu, n - 3)
                    if n == 7:
                        pe.wait_ge(iw_moved, 1)
                    rows = slice(HEAD * (h % 2), HEAD * (h % 2) + HEAD)
                    for c in range(0, P * (i + 1), HALF):
                        w = min(HALF, P * (i + 1) - c)
                        ins = pe.matmul(pair(n % 4)[:, c:c + w], iqT[rows, h // 2, i * P:(i + 1) * P],
                                        ikT[rows, c:c + w], start=True, stop=True)
                    ins.then_inc(idx_ready, 1)
                    n += 1
            for g in A_GROUPS:
                project(g)

            def scores(ph, s, m):
                b, i = place_of(ph, s)
                length = P * (i + 1)
                u = (ph * STEPS + s) * 2 + m
                if ph == 1 and bank_free[u] < 2 * STEPS or bank_free[u] < 0:
                    end = score_bank[u] + (1 if length <= HALF else 2)
                    pe.wait_ge(bank_moved, moved[(A_GROUPS, B_GROUPS)[ph][-1]] + end)
                if bank_free[u] >= 0:
                    pe.wait_ge(exp_done, bank_free[u] + 1)
                rows = slice(HEAD * m, HEAD * m + HEAD)
                masked = ph == 1 and i >= SEL0
                if masked:
                    pe.wait_ge(mask_made, TILES - SEL0)
                for c in range(0, length, HALF):
                    w = min(HALF, length - c)
                    o = score_of(u, c, c + w)
                    ins = pe.matmul(o, qT[rows, b, i * P:(i + 1) * P], kT[rows, b, c:c + w],
                                    start=True, stop=not masked)
                    if masked:
                        mk = mask[:, score_off[i] + c:score_off[i] + c + w]
                        ins = pe.matmul(o, identb[:, :], mk, start=False, stop=True)
                ins.then_inc(s_ready, 1)

            def turn(ph, s, quad):
                q, m, j, nj = quad
                if ph == 0:
                    pe.wait_ge(combined, s + 1)
                else:
                    pe.wait_ge(exp_done, (STEPS + s) * 2 + m + 1)
                if q >= 2:
                    wait_moved(q - 2)
                p = probs_of(ph, s, m)
                for k in range(nj):
                    ins = pe.transpose(bank(T_BANK + q % 2)[:, k * P:(k + 1) * P],
                                       p[:, (j + k) * P:(j + k + 1) * P], ident[:, :])
                ins.then_inc(t_ready, 1)

            def weigh(ph, s, quad):
                q, m, j, nj = quad
                b, i = place_of(ph, s)
                n = ph * STEPS + s
                if j == 0 and m == 0 and n >= 1:
                    pe.wait_ge(o_moved, n)
                wait_moved(q)
                if ph == 0:
                    cols, o = slice(b * P, (b + 1) * P), bank(O_BANK)[:, 0:P]
                else:
                    cols = slice(b * P + m * HEAD, b * P + (m + 1) * HEAD)
                    o = bank(O_BANK)[:, m * HEAD:(m + 1) * HEAD]
                for k in range(nj):
                    ins = pe.matmul(o, probsT[ph][:, q % 4, k * P:(k + 1) * P], v[:, j + k, cols],
                                    start=(j + k == 0), stop=(j + k == i))
                ins.then_inc(pv_done, 1)

            def attend(ph):
                lag = 1 if ph == 0 else 0
                scores(ph, 0, 0)
                scores(ph, 0, 1)
                for s in range(STEPS + lag):
                    t = s - lag
                    qs = quads[ph, t] if t >= 0 else []
                    if s + 1 < STEPS:
                        scores(ph, s + 1, 0)
                    if t == 0:
                        pe.wait_ge(bank_moved, moved[(A_GROUPS, B_GROUPS)[ph][-1] + 1])
                    for quad in qs[0:2]:
                        turn(ph, t, quad)
                    if s + 1 < STEPS:
                        scores(ph, s + 1, 1)
                    for k, quad in enumerate(qs):
                        if 2 <= k + 1 < len(qs):
                            turn(ph, t, qs[k + 1])
                        weigh(ph, t, quad)

            attend(0)
            for g in B_GROUPS:
                project(g)
            attend(1)

            def turn_mix(t):
                for half in range(2):
                    n = 2 * t + half
                    if t >= 2:
                        pe.wait_ge(mixT_lo, n - 3)
                    src = mixA if half == 0 else mixB
                    for c in range(4):
                        ins = pe.transpose(bank(n % 4)[:, c * P:(c + 1) * P], src[:, t, c * P:(c + 1) * P],
                                           ident[:, :])
                    ins.then_inc(mixT_ready, 1)

            pe.wait_ge(mixA_done, STEPS)
            pe.wait_ge(o_moved, 2 * STEPS)
            turn_mix(0)
            pe.wait_ge(w_lo_made, CHUNKS + 2 * DB)
            for t in range(TILES):
                if t + 1 < TILES:
                    turn_mix(t + 1)
                pe.wait_ge(mixT_lo, 2 * t + 2)
                if t >= 2:
                    pe.wait_ge(y_summed, t - 1)
                for half in range(2):
                    cols = slice(half * HALF, (half + 1) * HALF)
                    o = bank(4 + 2 * (t % 2) + half)
                    for e in range(DB):
                        for k, (a, w) in enumerate(((mx_hi, big_hi), (mx_hi, big_lo), (mx_lo, big_hi))):
                            ins = pe.matmul(o, a[:, t % 2, e, :], w[:, e, cols],
                                            start=(e == 0 and k == 0), stop=(e == DB - 1 and k == 2))
                ins.then_inc(y_ready, 1)

        @block.vector
        def _(dve):
            own = [0]

            def link(ins):
                own[0] += 1
                ins.then_inc(dve_own, 1)
                dve.wait_ge(dve_own, own[0])

            def inverse_root(root, var, done, a, b):
                link(dve.reciprocal(root, root))
                link(dve.tensor_tensor(a, root, root, ALU.mult))
                link(dve.tensor_tensor(a, a, var, ALU.mult))
                link(dve.tensor_scalar(a, a, -0.5, 1.5, ALU.mult, ALU.add))
                ins = dve.tensor_tensor(root, root, a, ALU.mult)
                if done is None:
                    link(ins)
                else:
                    ins.then_inc(done, 1)

            nh = A_HEADS + B_HEADS

            def low_h(n):
                half, d = divmod(n, DB)
                cols = slice(half * HALF, (half + 1) * HALF)
                dve.wait_ge(hT_hi, n + 1)
                dve.scalar_tensor_tensor(out=big_lo[:, d, cols], in0=bank(d), scalar=nw[:, d:d + 1],
                                         in1=big_hi[:, d, cols].bitcast(f32), op0=ALU.mult,
                                         op1=ALU.subtract).then_inc(hT_lo, 1)

            dve.memset(warm, 1.0).then_inc(warm_made, 1)
            dve.wait_ge(nw_turned, 1)
            dve.tensor_copy(nw[:, :], bank(7)[:, 0:DB]).then_inc(nw_moved, 1)
            EARLY = 0
            for t in range(0, TILES, 2):
                two = slice(t, t + 2)
                if t == TILES - 2:
                    for n in range(EARLY):
                        low_h(n)
                dve.wait_ge(x_squared, t + 2)
                dve.tensor_scalar(varx[:, two], ssx[:, two], 1.0 / D_MODEL, EPS, ALU.mult, ALU.add
                                  ).then_inc(x_var, 1)
                dve.wait_ge(x_root, t // 2 + 1)
                inverse_root(rstd[:, two], varx[:, two], x_rstd, t_a, None)
                dve.wait_ge(x_rstd, t // 2 + 1)
                dve.tensor_scalar(xs[:, t, :], xs[:, t, :], rstd[:, t:t + 1], None, ALU.mult
                                  ).then_inc(x_scaled[0], 1)
            for n in range(EARLY, 2 * DB):
                low_h(n)
            dve.wait_ge(consts_loaded, 16 * 5)
            for m in range(2):
                link(dve.tensor_tensor(lam4[:, 2 * m, :], lam4[:, 2 * m, :], lam4[:, 2 * m + 1, :], ALU.mult))
            for m in range(2):
                dve.reduce_sum(lam_s[:, m:m + 1], lam4[:, 2 * m, :], AX.X).then_inc(lam_sums, 1)
            for h in range(nh):
                dve.wait_ge(band_ready, h + 1)
                dve.tensor_copy(band[:, h, :], bank(6 + h % 2)[:, 0:RELS]).then_inc(band_out, 1)
            dve.wait_ge(bank_ready, 2)
            dve.tensor_copy(ikT[0:HEAD, HALF:SEQ], bank(1)[0:HEAD, :])
            dve.tensor_copy(ikT[HEAD:P, HALF:SEQ], bank(1)[0:HEAD, :])
            dve.tensor_scalar(iwT[:, HALF:SEQ], bank(1)[HEAD:HEAD + IDX_HEADS, :], IDX_SCALE, None, ALU.mult
                              ).then_inc(ik_moved, 1)
            dve.wait_ge(iw_ready, 1)
            dve.tensor_copy(iw[:, :], bank(7)[:, 0:TILES * IDX_HEADS]).then_inc(iw_moved, 1)
            dve.wait_ge(iw_moved, 1)
            n = 0
            for i in range(SEL0, TILES):
                sc = score[:, score_off[i]:score_off[i] + P * (i + 1)]
                for h in range(IDX_HEADS):
                    dve.wait_ge(idx_relu, n + 1)
                    r = relu[:, n % 2, 0:P * (i + 1)]
                    wcol = iw[:, i * IDX_HEADS + h:i * IDX_HEADS + h + 1]
                    if h == 0:
                        ins = dve.tensor_scalar(sc, r, wcol, None, ALU.mult)
                    else:
                        dve.wait_ge(idx_added, n)
                        ins = dve.scalar_tensor_tensor(out=sc, in0=r, scalar=wcol, in1=sc, op0=ALU.mult,
                                                       op1=ALU.add)
                    ins.then_inc(idx_added, 1)
                    n += 1
                dve.wait_ge(idx_added, n)
                link(dve.memset(score[0:CHUNK, score_off[i] + P * (i + 1) - CHUNK:
                                      score_off[i] + P * (i + 1)], UNSEEN))

            dve.wait_ge(lam_exp, 1)
            link(dve.tensor_tensor(neglam, lam_e[:, 1:2], lam_e[:, 0:1], ALU.subtract))
            link(dve.tensor_scalar(neglam, neglam, -LAMBDA_INIT, None, ALU.add))
            dve.wait_ge(bias_loaded, 16 * nh)
            link(dve.memset(bias[0:CHUNK, :, BAND - CHUNK:BAND], MASKED))

            def select(rounds):
                for _ in range(rounds):
                    for i in range(SEL0, TILES):
                        sc = score[:, score_off[i]:score_off[i] + P * (i + 1)]
                        ins = dve.max(top8[:, i - SEL0, :], sc)
                        if i == TILES - 1:
                            link(ins)
                    for i in range(SEL0, TILES):
                        sc = score[:, score_off[i]:score_off[i] + P * (i + 1)]
                        ins = dve.match_replace(sc, top8[:, i - SEL0, :], sc, TAKEN)
                        if i == TILES - 1:
                            link(ins)

            def soften(ph, s, m):
                b, i = place_of(ph, s)
                length = P * (i + 1)
                w = min(BAND, length)
                u = (ph * STEPS + s) * 2 + m
                h = b if ph == 0 else A_HEADS + 2 * b + m
                dve.wait_ge(s_ready, u + 1)
                least = UNSEEN_MIN
                if length > w:
                    least = farmin[:, u % 4:u % 4 + 1]
                    link(dve.tensor_reduce(least, score_of(u, 0, length - w), AX.X, ALU.min))
                o = score_of(u, length - w, length)
                dve.tensor_tensor_reduce(out=o, in0=o, in1=bias[:, h, BAND - w:BAND], scale=1.0,
                                         scalar=least, op0=ALU.add, op1=ALU.min,
                                         accum_out=negmax[:, u % 4:u % 4 + 1]).then_inc(max_ready, 1)

            def turned(ph, quads):
                for q, m, j, nj in quads:
                    if mover[q] == 1:
                        dve.wait_ge(t_ready, q + 1)
                        if q >= 4:
                            dve.wait_ge(pv_done, q - 3)
                        dve.tensor_copy(probsT[ph][:, q % 4, 0:nj * P], bank(T_BANK + q % 2)[:, 0:nj * P]
                                        ).then_inc(t_moved[1], 1)

            def factor(s):
                c = 2 * s % 8
                dve.wait_ge(exp_done, 2 * s + 2)
                link(dve.reciprocal(rinv[:, c:c + 2], rsum[:, c:c + 2]))
                link(dve.scalar_tensor_tensor(out=comb_c[:, s % 2:s % 2 + 1], in0=rsum[:, c:c + 1],
                                              scalar=neglam, in1=rinv[:, c + 1:c + 2], op0=ALU.mult,
                                              op1=ALU.mult))
                length = P * (place_of(0, s)[1] + 1)
                p1, p2 = (probs_of(0, s, m)[:, 0:length] for m in range(2))
                dve.scalar_tensor_tensor(out=p1, in0=p2, scalar=comb_c[:, s % 2:s % 2 + 1], in1=p1,
                                         op0=ALU.mult, op1=ALU.add).then_inc(combined, 1)

            def finishA(s):
                dve.wait_ge(pv_done, quads_through(0, s))
                if s >= 4:
                    dve.wait_ge(o_gated, s - 3)
                    dve.wait_ge(o_squared, s - 3)
                dve.tensor_scalar(o_tmp[:, s % 4, :], bank(O_BANK)[:, 0:P],
                                  rinv[:, 2 * s % 8:2 * s % 8 + 1], None, ALU.mult).then_inc(o_moved, 1)

            ROUNDS = TOPK // 8
            FIRST = ROUNDS // 2
            select(FIRST)
            soften(0, 0, 0)
            soften(0, 0, 1)
            for s in range(STEPS):
                if s >= 2:
                    finishA(s - 2)
                if s + 1 < STEPS:
                    soften(0, s + 1, 0)
                factor(s)
                if s + 1 < STEPS:
                    soften(0, s + 1, 1)
            finishA(STEPS - 2)
            finishA(STEPS - 1)
            dve.wait_ge(o_squared, STEPS)
            link(dve.tensor_scalar(ssA, ssA, 1.0 / P, EPS, ALU.mult, ALU.add))
            dve.tensor_copy(t_a[:, 0:1], ssA[:, 0:1]).then_inc(varA, 1)
            dve.wait_ge(rootA, 1)
            inverse_root(rA, ssA, rstdA, iw[:, 0:STEPS], None)
            select(ROUNDS - FIRST)
            for i in range(SEL0, TILES):
                o = slice(score_off[i], score_off[i] + P * (i + 1))
                dve.tensor_scalar(mask[:, o], score[:, o], TAKEN, MASKED, ALU.not_equal, ALU.mult
                                  ).then_inc(mask_made, 1)

            def finishB(s):
                b, i = place_of(1, s)
                n = STEPS + s
                c = (2 * n) % 8
                dve.wait_ge(exp_done, 2 * n + 2)
                link(dve.reciprocal(rinv[:, c:c + 2], rsum[:, c:c + 2]))
                dve.wait_ge(pv_done, quads_through(1, s))
                for m in range(2):
                    g = mixB[:, i, b * P + m * HEAD:b * P + (m + 1) * HEAD]
                    ins = dve.scalar_tensor_tensor(out=g, in0=bank(O_BANK)[:, m * HEAD:(m + 1) * HEAD],
                                                   scalar=rinv[:, c + m:c + m + 1], in1=g, op0=ALU.mult,
                                                   op1=ALU.mult)
                ins.then_inc(o_moved, 1)

            soften(1, 0, 0)
            soften(1, 0, 1)
            dve.wait_ge(bank_moved, moved[9])
            for s in range(STEPS + 1):
                qs = quads[1, s] if s < STEPS else []
                if s >= 1:
                    finishB(s - 1)
                if s + 1 < STEPS:
                    soften(1, s + 1, 0)
                turned(1, qs[0:2])
                if s + 1 < STEPS:
                    soften(1, s + 1, 1)
                turned(1, qs[2:])

            for t in range(TILES + 1):
                if t < TILES:
                    for half in range(2):
                        n = 2 * t + half
                        dve.wait_ge(mixT_hi, n + 1)
                        blk = slice(half * 4, half * 4 + 4)
                        dve.tensor_tensor(mx_lo[:, t % 2, blk, :],
                                          bank(n % 4)[:, :].rearrange("p (c q) -> p c q", q=P),
                                          mx_hi[:, t % 2, blk, :].bitcast(f32), ALU.subtract
                                          ).then_inc(mixT_lo, 1)
                if t >= 1:
                    k = t - 1
                    dve.wait_ge(y_ready, k + 1)
                    dve.wait_ge(xres_loaded[k % 2], 16 * (k // 2 + 1))
                    if k >= 2:
                        dve.wait_ge(y_squared, k - 1)
                        dve.wait_ge(y_scaled, k - 1)
                    dve.tensor_tensor(y[:, k % 2, :], pair(2 + k % 2), xres[:, k % 2, :], ALU.add
                                      ).then_inc(y_summed, 1)
                    dve.wait_ge(y_squared, k + 1)
                    dve.tensor_scalar(varx[:, k:k + 1], ssx[:, k:k + 1], 1.0 / D_MODEL, EPS, ALU.mult,
                                      ALU.add).then_inc(y_var, 1)
                    dve.wait_ge(y_root, k + 1)
                    inverse_root(rstd[:, k:k + 1], varx[:, k:k + 1], None, t_a[:, 0:1], None)
                    dve.wait_ge(fw_loaded, 16)
                    if k >= 2:
                        dve.wait_ge(stored[k % 2], 16 * (k // 2))
                    dve.scalar_tensor_tensor(out=y_out[:, k % 2, :], in0=y[:, k % 2, :],
                                             scalar=rstd[:, k:k + 1], in1=fw[:, :], op0=ALU.mult,
                                             op1=ALU.mult).then_inc(y_scaled, 1)


INPUTS = ["x", "norm_w", "w_in", "w_out", "lambda_q1", "lambda_k1", "lambda_q2", "lambda_k2",
          "subln_w", "rel_bias", "final_norm_w"]


def kernel(**inputs):
    import concourse.bacc as bacc
    from concourse.bass_utils import run_bass_kernel_spmd

    nc = bacc.Bacc("TRN2", target_bir_lowering=False, num_devices=1)
    f32 = mybir.dt.float32
    arrays, args = {}, []
    for name in INPUTS:
        arrays[f"in_{name}"] = np.ascontiguousarray(inputs[name])
    arrays["in_selector"] = bucket_selector()
    for name, a in arrays.items():
        args.append(nc.dram_tensor(name, a.shape, f32, kind="ExternalInput").ap())
    args.append(nc.dram_tensor("out_y", (1, SEQ, D_MODEL), f32, kind="ExternalOutput").ap())
    build(nc, *args)
    r = run_bass_kernel_spmd(nc, [arrays], core_ids=[0])
    return r.results[0]["out_y"]
```

```python
import math

import concourse.bass as bass
import numpy as np
from concourse import mybir

SEQ, D_MODEL = 1024, 1024
P = 128
CHUNK = 64
TILES = SEQ // P
DB = D_MODEL // P
WIDTH = 512
HALF = 512
HEAD = 64
BLOCKS = WIDTH // P
A_HEADS, B_HEADS = 4, 8
IDX_HEADS = 4
IDX_COL = 8 * WIDTH
IDX_COLS = IDX_HEADS * HEAD + HEAD + IDX_HEADS
TOPK = 256
SEL0 = TOPK // P
BUCKETS, MAX_DISTANCE = 32, 128
EPS = 1e-6
LAMBDA_INIT = 0.8 - 0.6 * math.exp(0.0)
QK_SCALE = HEAD ** -0.5
IDX_SCALE = IDX_HEADS ** -0.5 * HEAD ** -0.5
MASKED = 1e30
UNSEEN = -3e38
UNSEEN_MIN = 3e38
TAKEN = -2e38
REL0 = -(2 * P - 1)
RELS = 3 * P
BAND = 2 * P
SW = 3


def bucket_selector():
    rel = REL0 + np.arange(RELS)
    nb = BUCKETS // 2
    exact = nb // 2
    n = np.abs(rel)
    nf = np.maximum(n, 1).astype(np.float32)
    large = exact + (np.log(nf / np.float32(exact)) / np.float32(math.log(MAX_DISTANCE / exact))
                     * np.float32(nb - exact)).astype(np.int32)
    large = np.minimum(large, nb - 1)
    bucket = np.where(rel > 0, nb, 0) + np.where(n < exact, n, large)
    hot = np.zeros((BUCKETS, RELS), np.float32)
    hot[bucket, np.arange(RELS)] = 1.0
    hot[nb - 1, :] -= 1.0
    return -hot


def build(nc, x, norm_w, w_in, w_out, lambda_q1, lambda_k1, lambda_q2, lambda_k2, subln_w,
          rel_bias, final_norm_w, selector, out):
    f32, f32r, bf16 = mybir.dt.float32, mybir.dt.float32r, mybir.dt.bfloat16
    ALU, ACT, AX = mybir.AluOpType, mybir.ActivationFunctionType, mybir.AxisListType

    top = [(nc.sbuf_base + 63) // 64 * 64]

    def place(name, shape, dt, at=None):
        size = int(np.prod(shape[1:])) * (2 if dt == bf16 else 4)
        if at is None:
            at = top[0]
            top[0] += (size + 31) // 32 * 32
        return nc.alloc_sbuf_tensor_at(name, shape, dt, offset=at), at

    big_hi, big_hi_at = place("big_hi", [P, DB, SEQ], f32r)
    big_lo, big_lo_at = place("big_lo", [P, DB, SEQ], f32r)
    qT, qT_at = place("qT", [P, BLOCKS, SEQ], f32)
    kT, kT_at = place("kT", [P, BLOCKS, SEQ], f32)
    v, v_at = place("v", [P, TILES, WIDTH], f32)
    mixA, _ = place("mixA", [P, TILES, WIDTH], f32)
    score_at = top[0]
    score_off = {}
    total = 0
    for i in range(SEL0, TILES):
        score_off[i] = total
        total += P * (i + 1)
    score, _ = place("score", [P, max(total, TILES * WIDTH)], f32)
    mixB, _ = place("mixB", [P, TILES, WIDTH], f32, at=score_at)
    mask, mask_at = place("mask", [P, total], bf16)
    bias, bias_at = place("bias", [P, A_HEADS + B_HEADS, BAND], f32)
    w_raw, w_raw_at = place("w_raw", [P, SW, WIDTH], f32)
    probs, probs_at = place("probs", [P, 4, SEQ], f32)
    w_hi, w_hi_at = place("w_hi", [P, SW, WIDTH], f32r)
    w_lo, _ = place("w_lo", [P, SW, WIDTH], f32r)
    ident, _ = place("ident", [P, P], f32)
    identb, _ = place("identb", [P, P], bf16)
    subln, _ = place("subln", [P, P], f32)
    o_tmp, o_tmp_at = place("o_tmp", [P, 4, P], f32)
    sq_junk, _ = place("sq_junk", [P, P], bf16)
    nw, _ = place("nw", [P, DB], f32)
    probs_x, probs_x_at = place("probs_x", [P, 1, SEQ], f32)
    iw, _ = place("iw", [P, TILES * IDX_HEADS], f32)
    small, _ = place("small", [P, 128], f32)
    top8, _ = place("top8", [P, TILES - SEL0, 8], f32)
    assert top[0] <= nc.sbuf_usable_end, (top[0], nc.sbuf_usable_end)
    probsT = [place("probsT_A", [P, 4, HALF], f32, at=mask_at)[0],
              place("probsT_B", [P, 4, HALF], f32, at=w_hi_at)[0]]
    qT_r, _ = place("qT_r", [P, BLOCKS, SEQ], f32r, at=qT_at)
    kT_r, _ = place("kT_r", [P, BLOCKS, SEQ], f32r, at=kT_at)
    ROW = 4 * SEQ
    STACKS_AT = [[(w_raw_at + 4 * WIDTH, bias_at + ROW, bias_at + 2 * ROW),
                  (w_hi_at, w_hi_at + ROW, w_hi_at + 2 * ROW)],
                 [(w_raw_at + 4 * WIDTH, probs_x_at, bias_at),
                  (big_hi_at + 7 * ROW, big_lo_at + 7 * ROW, big_lo_at + 6 * ROW)]]
    stacks = [[[place(f"{name}_{ph}_{b}", [P, SEQ], f32r, at=at)[0]
                for name, at in zip(("q1_low_high", "k0_high_twice", "k1_high_twice"), STACKS_AT[ph][b])]
               for b in range(2)] for ph in range(2)]
    q_part, _ = place("q_part", [HEAD, HALF], f32r, at=o_tmp_at)
    w_tail, _ = place("w_tail", [P, 2, WIDTH], f32, at=w_hi_at + 2 * ROW)
    lam4, _ = place("lam4", [P, 4, HEAD], f32, at=mask_at + 4096)
    xs, _ = place("xs", [P, TILES, D_MODEL], f32, at=qT_at)
    x_junk, _ = place("x_junk", [P, D_MODEL], bf16, at=probs_at + 12 * 1024)
    iqT, _ = place("iqT", [P, 2, SEQ], f32, at=v_at)
    ikT, _ = place("ikT", [P, SEQ], f32, at=v_at + 8192)
    iwT, _ = place("iwT", [IDX_HEADS, SEQ], f32, at=mask_at)
    relu, _ = place("relu", [P, 2, SEQ], f32, at=probs_at)
    table, _ = place("table", [BUCKETS, A_HEADS + B_HEADS], f32, at=probs_at)
    nw8, _ = place("nw8", [DB, P], f32, at=probs_at + 8192)
    sel, _ = place("sel", [BUCKETS, RELS], f32, at=probs_at + 64)
    tableb, _ = place("tableb", [BUCKETS, A_HEADS + B_HEADS, P], f32, at=probs_at + 64 + 4 * RELS)
    band, _ = place("band", [P, A_HEADS + B_HEADS, RELS], f32, at=v_at + 12288)
    mx_hi, _ = place("mx_hi", [P, 2, DB, P], f32r, at=qT_at)
    mx_lo, _ = place("mx_lo", [P, 2, DB, P], f32r, at=qT_at + 8192)
    xres, _ = place("xres", [P, 2, D_MODEL], f32, at=kT_at)
    fw, _ = place("fw", [P, D_MODEL], f32, at=kT_at + 8192)
    y, _ = place("y", [P, 2, D_MODEL], f32, at=v_at)
    y_out, _ = place("y_out", [P, 2, D_MODEL], f32, at=v_at + 8192)
    y_junk, _ = place("y_junk", [P, D_MODEL], bf16, at=kT_at + 12288)

    rstd = small[:, 0:8]
    t_a = small[:, 8:10]
    warm = small[:, 126:127]
    ssx = small[:, 10:18]
    neglam = small[:, 18:19]
    lam_e = small[:, 20:22]
    negmax = small[:, 24:28]
    farmin = small[:, 80:84]
    rsum = small[:, 28:36]
    rinv = small[:, 36:44]
    comb_c = small[:, 44:46]
    ssA = small[:, 48:80]
    rA = small[:, 84:116]
    lam_s = small[:, 116:118]
    varx = small[:, 118:126]

    from contextlib import ExitStack
    ctx = ExitStack()
    with ctx:
        def sem(name):
            return ctx.enter_context(nc.semaphore(name))

        psum = ctx.enter_context(nc.psum_tensor("psum", [P, 8 * HALF], f32))
        scratch = nc.dram_tensor("bias_scratch", [P * (A_HEADS + B_HEADS) * RELS], f32, kind="Internal")

        def bank(n):
            return psum[:, n * HALF:(n + 1) * HALF]

        def pair(n):
            return psum[:, n * 2 * HALF:(n + 1) * 2 * HALF]

        x_loaded = [sem(f"x_loaded{t}") for t in range(TILES)]
        consts_loaded = sem("consts_loaded")
        table_loaded = sem("table_loaded")
        nw_loaded = sem("nw_loaded")
        nw_turned = sem("nw_turned")
        nw_moved = sem("nw_moved")
        band_stored = sem("band_stored")
        bias_loaded = sem("bias_loaded")
        w_loaded = [sem(f"w_loaded{r}") for r in range(SW)]
        xres_loaded = [sem(f"xres_loaded{r}") for r in range(2)]
        fw_loaded = sem("fw_loaded")
        stored = [sem(f"stored{r}") for r in range(2)]
        consts_made = sem("consts_made")
        x_squared = sem("x_squared")
        x_var = sem("x_var")
        x_root = sem("x_root")
        x_rstd = sem("x_rstd")
        x_scaled = [sem("x_scaled_dve"), sem("x_scaled_pool")]
        warm_made = sem("warm_made")
        hT_ready = sem("hT_ready")
        hT_hi = sem("hT_hi")
        hT_lo = sem("hT_lo")
        lam_sums = sem("lam_sums")
        lam_exp = sem("lam_exp")
        tableb_made = sem("tableb_made")
        band_ready = sem("band_ready")
        band_out = sem("band_out")
        w_hi_made = sem("w_hi_made")
        w_lo_made = sem("w_lo_made")
        chunk_used = sem("chunk_used")
        bank_ready = sem("bank_ready")
        bank_moved = sem("bank_moved")
        ik_moved = sem("ik_moved")
        iw_ready = sem("iw_ready")
        iw_moved = sem("iw_moved")
        idx_ready = sem("idx_ready")
        idx_relu = sem("idx_relu")
        idx_added = sem("idx_added")
        mask_made = sem("mask_made")
        s_ready = sem("s_ready")
        max_ready = sem("max_ready")
        exp_done = sem("exp_done")
        combined = sem("combined")
        t_ready = sem("t_ready")
        t_moved = [sem("t_moved_act"), sem("t_moved_dve")]
        pv_done = sem("pv_done")
        o_moved = sem("o_moved")
        o_squared = sem("o_squared")
        o_gated = sem("o_gated")
        kh_made = sem("kh_made")
        kh_copied = [sem(f"kh_copied{r}") for r in range(2)]
        split = sem("split")
        rootA = sem("rootA")
        varA = sem("varA")
        rstdA = sem("rstdA")
        mixA_done = sem("mixA_done")
        wout_hi = sem("wout_hi")
        mixT_ready = sem("mixT_ready")
        mixT_hi = sem("mixT_hi")
        mixT_lo = sem("mixT_lo")
        y_ready = sem("y_ready")
        y_summed = sem("y_summed")
        y_squared = sem("y_squared")
        y_var = sem("y_var")
        y_root = sem("y_root")
        y_scaled = sem("y_scaled")
        dve_own = sem("dve_own")
        pool_own = sem("pool_own")

        GROUPS = [(IDX_COL, IDX_COLS, "T")]
        for g in range(2):
            for n in range(4):
                GROUPS.append(((4 * g + n) * WIDTH, WIDTH, "T" if n < 2 else "N"))
        banks = [6] + [8] * 8
        before = [sum(banks[:g]) for g in range(10)]
        moved = [0] + [n - 1 for n in before[1:]]
        A_GROUPS, B_GROUPS = range(1, 5), range(5, 9)
        CHUNKS = len(GROUPS) * DB

        ORDER = ([2, 4, 6, 7, 5, 3, 1, 0], [3, 5, 2, 0, 1, 4, 6, 7])
        STEPS = BLOCKS * TILES

        def place_of(ph, s):
            return s // TILES, ORDER[ph][s % TILES]

        quads = {}
        n = 0
        for ph in range(2):
            for s in range(STEPS):
                nb = place_of(ph, s)[1] + 1
                quads[ph, s] = []
                for m in ([0] if ph == 0 else [0, 1]):
                    for j in range(0, nb, 4):
                        quads[ph, s].append((n, m, j, min(4, nb - j)))
                        n += 1

        def probs_of(ph, s, m):
            if ph == 1:
                return probs[:, (2 * s + m) % 4, :]
            if m == 0:
                return probs[:, s % 3, :]
            return probs[:, 3, :] if s % 2 == 0 else probs_x[:, 0, :]

        S_BANKS, O_BANK, T_BANK = 5, 5, 6
        score_bank, bank_free = {}, {}
        last = [-1] * S_BANKS
        for u in range(4 * STEPS):
            need = 1 if place_of(u // (2 * STEPS), u // 2 % STEPS)[1] < HALF // P else 2
            first = min(range(S_BANKS - need + 1), key=lambda k: (max(last[k:k + need]), k))
            score_bank[u], bank_free[u] = first, max(last[first:first + need])
            last[first:first + need] = [u] * need

        def score_of(u, c0, c1):
            return psum[:, score_bank[u] * HALF + c0:score_bank[u] * HALF + c1]

        quads_A = quads[0, STEPS - 1][-1][0] + 1
        mover, moves = {}, {}
        for q in range(n):
            mover[q] = q % 2 if q >= quads_A else 0
            moves[q] = sum(mover[k] == mover[q] for k in range(q + 1))

        def wait_moved(q):
            nc.tensor.wait_ge(t_moved[mover[q]], moves[q])

        def quads_through(ph, s):
            return quads[ph, s][-1][0] + 1

        def column_block(g, t):
            c, half = divmod(t, 2)
            return ((2, 0, 1)[c] if g == 0 else c), half

        def wait_chunk_used(eng, n):
            g, d = divmod(n, DB)
            if d == DB - 1:
                eng.wait_ge(bank_ready, before[g + 1])
            else:
                eng.wait_ge(chunk_used, g * (DB - 1) + d + 1)

        def w_staged(n):
            r = n % SW
            return w_raw[:, r, :] if n < CHUNKS or r == 0 else w_tail[:, r - 1, :]

        def units_before(ph, b):
            return 2 * (ph * STEPS + b * TILES)

        LATE = CHUNKS + 12

        block = ctx.enter_context(nc.Block())

        @block.sync
        def _(sp):
            for t in range(TILES):
                sp.dma_start(xs[:, t, :], x[0, t * P:(t + 1) * P, :]).then_inc(x_loaded[t], 16)
                if t == 0:
                    sp.dma_start(nw8[:, :], norm_w.rearrange("o (c p) -> (o c) p", p=P)).then_inc(nw_loaded, 16)
                    sp.dma_start(table[:, :], rel_bias).then_inc(table_loaded, 16)
                    sp.dma_start(sel[:, :], selector).then_inc(table_loaded, 16)

            def load_chunk(n):
                if n >= SW:
                    sp.wait_ge(w_lo_made, n - SW + 1)
                if n < CHUNKS:
                    c0, cols, _ = GROUPS[n // DB]
                    d = n % DB
                    src = w_in[0, d * P:(d + 1) * P, c0:c0 + cols]
                else:
                    d, half = divmod(n - CHUNKS, 2)
                    cols = WIDTH
                    src = w_out[0, d * P:(d + 1) * P, half * WIDTH:(half + 1) * WIDTH]
                sp.dma_start(w_staged(n)[:, 0:cols], src).then_inc(w_loaded[n % SW], 16)

            for n in range(DB + SW):
                load_chunk(n)
                if n == 0:
                    sp.dma_start(subln[:, :], subln_w.to_broadcast([P, P])).then_inc(consts_loaded, 16)
                    for k, row in enumerate((lambda_q1, lambda_k1, lambda_q2, lambda_k2)):
                        sp.dma_start(lam4[:, k, :], row.to_broadcast([P, HEAD])).then_inc(consts_loaded, 16)
            nh = A_HEADS + B_HEADS
            sp.wait_ge(band_out, nh)
            sp.dma_start(bass.AP(scratch, 0, [[nh * RELS, P], [1, nh * RELS]]),
                         band[:, :, :].rearrange("p h r -> p (h r)")).then_inc(band_stored, 16)
            sp.wait_ge(band_stored, 16)

            def load_bias(h):
                sp.dma_start(bias[:, h, :],
                             bass.AP(scratch, h * RELS + P - 1, [[nh * RELS - 1, P], [1, BAND]])
                             ).then_inc(bias_loaded, 16)

            def copy_keys(ph, b):
                _, k0, k1 = stacks[ph][b % 2]
                sp.wait_ge(kh_made, ph * BLOCKS + b + 1)
                sp.dma_start(k0[HEAD:P, :].bitcast(f32), k0[0:HEAD, :].bitcast(f32)).then_inc(kh_copied[b % 2], 16)
                sp.dma_start(k1[0:HEAD, :].bitcast(f32), k1[HEAD:P, :].bitcast(f32)).then_inc(kh_copied[b % 2], 16)

            for h in range(A_HEADS):
                load_bias(h)
            for n in range(DB + SW, B_GROUPS[0] * DB):
                load_chunk(n)
            for b in range(BLOCKS):
                copy_keys(0, b)
            sp.wait_ge(s_ready, units_before(0, BLOCKS - 1))
            for n in range(B_GROUPS[0] * DB, B_GROUPS[0] * DB + SW):
                load_chunk(n)
            for h in range(A_HEADS, nh):
                load_bias(h)
            for n in range(B_GROUPS[0] * DB + SW, CHUNKS):
                load_chunk(n)
            copy_keys(1, 0)
            load_chunk(CHUNKS)
            wait_chunk_used(sp, CHUNKS - 1)
            load_chunk(CHUNKS + 1)
            load_chunk(CHUNKS + 2)
            copy_keys(1, 1)
            for n in range(CHUNKS + 3, CHUNKS + 9):
                load_chunk(n)
            copy_keys(1, 2)
            for n in range(CHUNKS + 9, CHUNKS + 15):
                load_chunk(n)
            copy_keys(1, 3)
            load_chunk(CHUNKS + 15)
            sp.wait_ge(pv_done, quads_through(1, STEPS - 1))
            sp.dma_start(fw[:, :], final_norm_w.rearrange("(o n) -> o n", o=1).to_broadcast([P, D_MODEL])
                         ).then_inc(fw_loaded, 16)
            for t in range(TILES + 1):
                if t < TILES:
                    if t >= 2:
                        sp.wait_ge(y_summed, 2 * t - 2)
                    sp.dma_start(xres[:, t % 2, :], x[0, t * P:(t + 1) * P, :]
                                 ).then_inc(xres_loaded[t % 2], 16)
                if t >= 1:
                    for half in range(2):
                        cols = slice(half * HALF, (half + 1) * HALF)
                        sp.wait_ge(y_scaled, 2 * t + half - 1)
                        sp.dma_start(out[0, (t - 1) * P:t * P, cols], y_out[:, (t - 1) % 2, cols]
                                     ).then_inc(stored[(t - 1) % 2], 16)
            sp.wait_ge(stored[0], 16 * TILES)
            sp.wait_ge(stored[1], 16 * TILES)

        @block.gpsimd
        def _(pool):
            own = [0]

            def link(ins):
                own[0] += 1
                ins.then_inc(pool_own, 1)
                pool.wait_ge(pool_own, own[0])

            for tile in (ident, identb):
                link(pool.memset(tile[:, :], 0.0))
                pool.affine_select(out=tile[:, :], in_=tile[:, :], compare_op=ALU.not_equal, fill=1.0,
                                   base=0, pattern=[[-1, P]], channel_multiplier=1
                                   ).then_inc(consts_made, 1)
            link(pool.memset(tableb[:, :, :], 1.0))
            for t in range(1, TILES, 2):
                pool.wait_ge(x_rstd, t // 2 + 1)
                pool.tensor_scalar(xs[:, t, :], xs[:, t, :], rstd[:, t:t + 1], 0.0, ALU.mult, ALU.add
                                   ).then_inc(x_scaled[1], 1)
                if t == 3:
                    pool.wait_ge(table_loaded, 32)
                    for h in range(A_HEADS + B_HEADS):
                        ins = pool.tensor_scalar(tableb[:, h, :], tableb[:, h, :], table[:, h:h + 1], 0.0,
                                                 ALU.mult, ALU.add)
                    ins.then_inc(tableb_made, 1)

            def low(n):
                cols = GROUPS[n // DB][1]
                pool.wait_ge(w_hi_made, n + 1)
                r = n % SW
                pool.tensor_tensor(w_lo[:, r, 0:cols], w_raw[:, r, 0:cols],
                                   w_hi[:, r, 0:cols].bitcast(f32), ALU.subtract
                                   ).then_inc(w_lo_made, 1)

            def rounded(out, src):
                return pool.tensor_scalar(out, src, 1.0, 0.0, ALU.mult, ALU.add)

            def rest(out, src, high):
                return pool.tensor_tensor(out, src, high.bitcast(f32), ALU.subtract)

            def split_q(ph, b, half):
                c = slice(half * HALF, (half + 1) * HALF)
                q1, k0, _ = stacks[ph][b % 2]
                part = q_part[:, :] if b == 0 else k0[0:HEAD, c]
                link(rounded(q1[HEAD:P, c], qT[HEAD:P, b, c]))
                link(rest(q1[0:HEAD, c], qT[HEAD:P, b, c], q1[HEAD:P, c]))
                link(rounded(part, qT[0:HEAD, b, c]))
                link(rest(qT_r[HEAD:P, b, c], qT[0:HEAD, b, c], part))
                ins = rounded(qT_r[0:HEAD, b, c], qT[0:HEAD, b, c])
                if half == 1:
                    ins.then_inc(split, 1)
                    pool.wait_ge(split, ph * BLOCKS + b + 1)
                else:
                    link(ins)

            def split_k(ph, b, half):
                c = slice(half * HALF, (half + 1) * HALF)
                _, k0, k1 = stacks[ph][b % 2]
                link(rounded(k0[0:HEAD, c], kT[0:HEAD, b, c]))
                link(rounded(k1[HEAD:P, c], kT[HEAD:P, b, c]))
                link(rest(kT_r[0:HEAD, b, c], kT[0:HEAD, b, c], k0[0:HEAD, c]))
                ins = rest(kT_r[HEAD:P, b, c], kT[HEAD:P, b, c], k1[HEAD:P, c])
                if half == 1:
                    ins.then_inc(kh_made, 1)
                    pool.wait_ge(kh_made, ph * BLOCKS + b + 1)
                else:
                    link(ins)

            def split_part(ph, b, j):
                if j == 0 and b == 1:
                    wait_chunk_used(pool, (A_GROUPS, B_GROUPS)[ph][-1] * DB + DB - 1)
                elif j == 0:
                    pool.wait_ge(s_ready, units_before(ph, b - 1))
                (split_q, split_q, split_k, split_k)[j](ph, b, j % 2)

            def project_low(ph):
                last = (A_GROUPS, B_GROUPS)[ph][-1]
                for d in range(DB):
                    low(last * DB + d)
                    if d in (1, 3, DB - 1):
                        pool.wait_ge(w_lo_made, last * DB + d + 1)
                    if d in (1, 3):
                        pool.wait_ge(bank_moved, moved[last - 1])
                        split_k(ph, 0, (d - 1) // 2)
                split_q(ph, 0, 0)
                split_q(ph, 0, 1)

            for n in range(A_GROUPS[-1] * DB):
                low(n)
            project_low(0)
            split_part(0, 1, 0)
            split_part(0, 1, 1)
            for s in range(STEPS):
                b, i = place_of(0, s)
                g = mixA[:, i, b * P:(b + 1) * P]
                if s == 0:
                    pool.wait_ge(bank_moved, moved[B_GROUPS[0]])
                pool.wait_ge(o_moved, s + 1)
                pool.tensor_tensor(g, g, o_tmp[:, s % 4, :], ALU.mult).then_inc(o_gated, 1)
                if (s + 2) % TILES < 4 and s + 2 < 3 * TILES:
                    pool.wait_ge(o_gated, s + 1)
                if s < 2:
                    split_part(0, 1, s + 2)
                elif (s + 2) % TILES < 4 and s + 2 < 3 * TILES:
                    split_part(0, (s + 2) // TILES + 1, (s + 2) % TILES)
                if s == STEPS - 4:
                    low(B_GROUPS[0] * DB)
            pool.wait_ge(consts_loaded, 16 * 5)
            link(pool.tensor_scalar(subln[:, :], subln[:, :], 1.0 - LAMBDA_INIT, 0.0, ALU.mult, ALU.add))
            for n in range(B_GROUPS[0] * DB + 1, B_GROUPS[-1] * DB):
                low(n)
                if n in (B_GROUPS[1] * DB, B_GROUPS[1] * DB + 4, B_GROUPS[2] * DB, B_GROUPS[2] * DB + 4):
                    if n == B_GROUPS[1] * DB:
                        pool.wait_ge(rstdA, 1)
                        pool.wait_ge(o_gated, STEPS)
                    block_b = (n - B_GROUPS[1] * DB) // 4
                    steps = range(block_b * TILES, (block_b + 1) * TILES)
                    for s in steps:
                        b, i = place_of(0, s)
                        g = mixA[:, i, b * P:(b + 1) * P]
                        ins = pool.tensor_scalar(g, g, rA[:, s:s + 1], 0.0, ALU.mult, ALU.add)
                    link(ins)
                    for s in steps:
                        b, i = place_of(0, s)
                        g = mixA[:, i, b * P:(b + 1) * P]
                        pool.tensor_tensor(g, g, subln[:, :], ALU.mult).then_inc(mixA_done, 1)
            project_low(1)

            def w_out_parts(n):
                d, half = divmod(n - CHUNKS, 2)
                dst = slice(half * WIDTH, (half + 1) * WIDTH)
                pool.wait_ge(w_loaded[n % SW], 16 * (n // SW + 1))
                pool.tensor_scalar(big_hi[:, d, dst], w_staged(n), 1.0, 0.0, ALU.mult, ALU.add
                                   ).then_inc(wout_hi, 1)
                pool.wait_ge(wout_hi, n - CHUNKS + 1)
                pool.tensor_tensor(big_lo[:, d, dst], w_staged(n),
                                   big_hi[:, d, dst].bitcast(f32), ALU.subtract).then_inc(w_lo_made, 1)

            for b in range(1, BLOCKS):
                for j in range(4):
                    split_part(1, b, j)
                if b < BLOCKS - 1:
                    for n in range(CHUNKS + 6 * (b - 1), CHUNKS + 6 * b):
                        w_out_parts(n)
                    pool.wait_ge(w_lo_made, CHUNKS + 6 * b)
            pool.wait_ge(s_ready, 4 * STEPS)
            for n in range(LATE, CHUNKS + 2 * DB):
                w_out_parts(n)

        @block.scalar
        def _(act):
            act.wait_ge(warm_made, 1)
            act.activation(warm, warm, ACT.Sqrt)
            def high(n):
                cols = GROUPS[n // DB][1]
                act.wait_ge(w_loaded[n % SW], 16 * (n // SW + 1))
                if n >= SW:
                    wait_chunk_used(act, n - SW)
                act.activation(w_hi[:, n % SW, 0:cols], w_raw[:, n % SW, 0:cols], ACT.Copy
                               ).then_inc(w_hi_made, 1)

            def high_h(n):
                half, d = divmod(n, DB)
                act.wait_ge(hT_ready, n + 1)
                act.activation(big_hi[:, d, half * HALF:(half + 1) * HALF], bank(d), ACT.Copy,
                               scale=nw[:, d:d + 1]).then_inc(hT_hi, 1)

            for t in range(TILES):
                act.wait_ge(x_loaded[t], 16)
                if t >= 1:
                    act.wait_ge(x_squared, t)
                act.activation(x_junk[:, :], xs[:, t, :], ACT.Square, accum_out=ssx[:, t:t + 1]
                               ).then_inc(x_squared, 1)
                if t == TILES - 1:
                    act.wait_ge(nw_moved, 1)
                    high_h(0)
                if t % 2 == 1:
                    act.wait_ge(x_var, t // 2 + 1)
                    act.activation(rstd[:, t - 1:t + 1], varx[:, t - 1:t + 1], ACT.Sqrt).then_inc(x_root, 1)
            for n in range(1, 2 * DB):
                high_h(n)
                if n in (DB - 1, DB, DB + 2):
                    high({DB - 1: 0, DB: 1, DB + 2: 2}[n])

            def move(g):
                kind = GROUPS[g][2]
                for t in range(banks[g]):
                    if g == 0 and t == 1:
                        continue
                    act.wait_ge(bank_ready, before[g] + t + 1)
                    c, half = column_block(g, t)
                    cols = slice(half * HALF, (half + 1) * HALF)
                    if g == 0:
                        if c < 2:
                            ins = act.activation(iqT[:, c, cols], bank(t), ACT.Copy)
                        else:
                            act.activation(ikT[0:HEAD, cols], bank(t)[0:HEAD, :], ACT.Copy)
                            act.activation(ikT[HEAD:P, cols], bank(t)[0:HEAD, :], ACT.Copy)
                            ins = act.activation(iwT[:, cols], bank(t)[HEAD:HEAD + IDX_HEADS, :],
                                                 ACT.Copy, scale=IDX_SCALE)
                    elif kind == "T":
                        is_q = g in (A_GROUPS[0], B_GROUPS[0])
                        ins = act.activation((qT if is_q else kT)[:, c, cols], bank(t), ACT.Copy,
                                             scale=-QK_SCALE if is_q else 1.0)
                    elif g in (A_GROUPS[2], B_GROUPS[2]):
                        ins = act.activation(v[:, t, :], bank(t), ACT.Copy)
                    else:
                        if g == B_GROUPS[3] and t == 0:
                            act.wait_ge(mask_made, TILES - SEL0)
                        ins = act.activation((mixA if g == A_GROUPS[3] else mixB)[:, t, :], bank(t),
                                             ACT.Silu)
                    ins.then_inc(bank_moved, 1)

            def project(groups, last):
                for g in groups:
                    for d in range(DB):
                        if g * DB + d >= started[0]:
                            high(g * DB + d)
                        if d == 1 and g > groups[0]:
                            move(g - 1)
                    started[0] = max(started[0], (g + 1) * DB)
                if last:
                    move(groups[-1])

            started = [3]
            project([0], False)
            high(DB)
            high(DB + 1)
            started[0] = DB + 2
            move(0)
            n = 0
            for i in range(SEL0, TILES):
                for h in range(IDX_HEADS):
                    act.wait_ge(idx_ready, n + 1)
                    if n >= 2:
                        act.wait_ge(idx_added, n - 1)
                    act.activation(relu[:, n % 2, 0:P * (i + 1)], pair(n % 4)[:, 0:P * (i + 1)],
                                   ACT.Relu).then_inc(idx_relu, 1)
                    n += 1
            act.wait_ge(lam_sums, 2)
            act.activation(lam_e, lam_s, ACT.Exp).then_inc(lam_exp, 1)

            project(list(A_GROUPS), True)

            def exp(ph, s, m):
                length = P * (place_of(ph, s)[1] + 1)
                u = (ph * STEPS + s) * 2 + m
                act.wait_ge(max_ready, u + 1)
                if ph == 0 and m == 0 and s >= 3:
                    act.wait_ge(t_ready, quads_through(0, s - 3))
                if ph == 0 and m == 1 and s >= 2:
                    act.wait_ge(combined, s - 1)
                if ph == 1 and s >= 2:
                    act.wait_ge(t_ready, [q for q, k, _, _ in quads[1, s - 2] if k == m][-1] + 1)
                act.activation(probs_of(ph, s, m)[:, 0:length], score_of(u, 0, length), ACT.Exp,
                               bias=negmax[:, u % 4:u % 4 + 1], scale=-1.0,
                               accum_out=rsum[:, u % 8:u % 8 + 1]).then_inc(exp_done, 1)

            def turned(ph, quads):
                for q, m, j, nj in quads:
                    if mover[q] == 0:
                        act.wait_ge(t_ready, q + 1)
                        if q >= 4:
                            act.wait_ge(pv_done, q - 3)
                        act.activation(probsT[ph][:, q % 4, 0:nj * P], bank(T_BANK + q % 2)[:, 0:nj * P], ACT.Copy
                                       ).then_inc(t_moved[0], 1)

            def finish(s):
                if s >= 1:
                    act.wait_ge(o_squared, s)
                act.wait_ge(o_moved, s + 1)
                act.activation(sq_junk[:, :], o_tmp[:, s % 4, :], ACT.Square,
                               accum_out=ssA[:, s:s + 1]).then_inc(o_squared, 1)

            exp(0, 0, 0)
            exp(0, 0, 1)
            for s in range(STEPS + 2):
                qs = quads[0, s - 1] if 1 <= s <= STEPS else []
                turned(0, qs)
                if s + 1 < STEPS:
                    exp(0, s + 1, 0)
                if s >= 2:
                    finish(s - 2)
                if s + 1 < STEPS:
                    exp(0, s + 1, 1)
                if s == STEPS - 1:
                    high(B_GROUPS[0] * DB)
            high(B_GROUPS[0] * DB + 1)
            high(B_GROUPS[0] * DB + 2)
            started[0] = B_GROUPS[0] * DB + SW
            act.wait_ge(varA, 1)
            act.activation(rA, ssA, ACT.Sqrt).then_inc(rootA, 1)
            project(list(B_GROUPS), True)

            exp(1, 0, 0)
            exp(1, 0, 1)
            for s in range(STEPS):
                qs = quads[1, s]
                turned(1, qs[0:2])
                if s + 1 < STEPS:
                    exp(1, s + 1, 0)
                turned(1, qs[2:3])
                if s + 1 < STEPS:
                    exp(1, s + 1, 1)
                turned(1, qs[3:])

            for t in range(TILES + 1):
                if t < TILES:
                    for half in range(2):
                        n = 2 * t + half
                        act.wait_ge(mixT_ready, n + 1)
                        if t >= 2:
                            act.wait_ge(y_ready, 2 * t - 2)
                        act.activation(mx_hi[:, t % 2, half * 4:half * 4 + 4, :],
                                       bank(n % 4)[:, :].rearrange("p (c q) -> p c q", q=P), ACT.Copy
                                       ).then_inc(mixT_hi, 1)
                if t >= 1:
                    for half in range(2):
                        n = 2 * (t - 1) + half
                        act.wait_ge(y_summed, n + 1)
                        if n >= 1:
                            act.wait_ge(y_squared, n)
                        act.activation(y_junk[:, 0:HALF], y[:, (t - 1) % 2, half * HALF:(half + 1) * HALF],
                                       ACT.Square, accum_out=ssA[:, n:n + 1]).then_inc(y_squared, 1)
                    act.wait_ge(y_var, t)
                    act.activation(rstd[:, t - 1:t], varx[:, t - 1:t], ACT.Sqrt).then_inc(y_root, 1)

        @block.tensor
        def _(pe):
            pe.wait_ge(consts_made, 2)
            pe.wait_ge(nw_loaded, 16)
            pe.transpose(bank(7)[:, 0:DB], nw8[:, :], ident[0:DB, 0:DB]).then_inc(nw_turned, 1)
            def turn_x(tt, d):
                ins = pe.transpose(bank(d)[:, tt % 4 * P:(tt % 4 + 1) * P],
                                   xs[:, tt, d * P:(d + 1) * P], ident[:, :])
                if tt % 4 == 3:
                    ins.then_inc(hT_ready, 1)

            for tt in range(4):
                pe.wait_ge(x_scaled[tt % 2], tt // 2 + 1)
                for d in range(DB):
                    if tt == 0 and d == DB - 1:
                        pe.wait_ge(nw_moved, 1)
                    turn_x(tt, d)
            for d in range(DB):
                pe.wait_ge(hT_lo, d + 1)
                for tt in range(4, TILES):
                    if d == 0:
                        pe.wait_ge(x_scaled[tt % 2], tt // 2 + 1)
                    turn_x(tt, d)

            def bias_row(h):
                pe.wait_ge(tableb_made, 1)
                pe.wait_ge(hT_lo, 2 * DB)
                if h >= 2:
                    pe.wait_ge(band_out, h - 1)
                pe.matmul(bank(6 + h % 2)[:, 0:RELS], tableb[:, h, :], sel[:, :], start=True, stop=True
                          ).then_inc(band_ready, 1)

            def project(g):
                c0, cols, kind = GROUPS[g]
                for d in range(DB):
                    n = g * DB + d
                    r = n % SW
                    pe.wait_ge(w_lo_made, n + 1)
                    if g == 0:
                        pe.wait_ge(hT_lo, DB + d + 1)
                    for t in range(banks[g]):
                        if d == 0 and g == A_GROUPS[0]:
                            pe.wait_ge(idx_relu, (TILES - SEL0) * IDX_HEADS - 3 + t // 2)
                        elif d == 0 and g == B_GROUPS[0]:
                            if t == O_BANK:
                                pe.wait_ge(o_moved, STEPS)
                            elif t >= T_BANK:
                                wait_moved(quads_A - 1)
                        elif d == 0 and g > 0:
                            pe.wait_ge(bank_moved, moved[g - 1] + t + 1)
                        if g == 0 and d == 0:
                            pe.wait_ge(hT_lo, DB + t + 1)
                        if kind == "T":
                            c, half = column_block(g, t)
                            m = min(P, cols - c * P)
                            ws = slice(c * P, c * P + m)
                            hs = slice(half * HALF, (half + 1) * HALF)
                            o = bank(t)[0:m, :]
                            passes = [(w_hi[:, r, ws], big_hi[:, d, hs]), (w_hi[:, r, ws], big_lo[:, d, hs]),
                                      (w_lo[:, r, ws], big_hi[:, d, hs])]
                        else:
                            hs = slice(t * P, (t + 1) * P)
                            o = bank(t)
                            passes = [(big_hi[:, d, hs], w_hi[:, r, :]), (big_hi[:, d, hs], w_lo[:, r, :]),
                                      (big_lo[:, d, hs], w_hi[:, r, :])]
                        for k, (a, b) in enumerate(passes):
                            ins = pe.matmul(o, a, b, start=(d == 0 and k == 0),
                                            stop=(d == DB - 1 and k == 2))
                        if d == DB - 1:
                            ins.then_inc(bank_ready, 1)
                    if d < DB - 1:
                        ins.then_inc(chunk_used, 1)
                    if g == 0 and 1 <= d <= 6:
                        bias_row(2 * d - 2)
                        bias_row(2 * d - 1)

            project(0)
            n = 0
            for i in range(SEL0, TILES):
                for h in range(IDX_HEADS):
                    if n == 0:
                        pe.wait_ge(bank_moved, 3)
                        pe.wait_ge(ik_moved, 1)
                    elif n == 2:
                        pe.wait_ge(bank_moved, moved[1])
                    elif n == 3:
                        pe.wait_ge(band_out, A_HEADS + B_HEADS)
                        for t in range(TILES):
                            ins = pe.transpose(bank(7)[:, 4 * t:4 * t + 4], iwT[:, t * P:(t + 1) * P],
                                               ident[0:IDX_HEADS, 0:IDX_HEADS])
                        ins.then_inc(iw_ready, 1)
                    elif n >= 4:
                        pe.wait_ge(idx_relu, n - 3)
                    if n == 7:
                        pe.wait_ge(iw_moved, 1)
                    rows = slice(HEAD * (h % 2), HEAD * (h % 2) + HEAD)
                    for c in range(0, P * (i + 1), HALF):
                        w = min(HALF, P * (i + 1) - c)
                        ins = pe.matmul(pair(n % 4)[:, c:c + w], iqT[rows, h // 2, i * P:(i + 1) * P],
                                        ikT[rows, c:c + w], start=True, stop=True)
                    ins.then_inc(idx_ready, 1)
                    n += 1
            for g in A_GROUPS:
                project(g)

            def scores(ph, s, m):
                b, i = place_of(ph, s)
                length = P * (i + 1)
                u = (ph * STEPS + s) * 2 + m
                if ph == 1 and bank_free[u] < 2 * STEPS or bank_free[u] < 0:
                    end = score_bank[u] + (1 if length <= HALF else 2)
                    pe.wait_ge(bank_moved, moved[(A_GROUPS, B_GROUPS)[ph][-1]] + end)
                if bank_free[u] >= 0:
                    pe.wait_ge(exp_done, bank_free[u] + 1)
                rows = slice(HEAD * m, HEAD * m + HEAD)
                if s % TILES == 0 and m == 0:
                    pe.wait_ge(kh_made, ph * BLOCKS + b + 1)
                    pe.wait_ge(kh_copied[b % 2], 32 * (ph * BLOCKS // 2 + b // 2 + 1))
                    pe.wait_ge(split, ph * BLOCKS + b + 1)
                q1, k0, k1 = stacks[ph][b % 2]
                q, k = (qT_r[:, b, :], k0) if m == 0 else (q1, k1)
                qt = slice(i * P, (i + 1) * P)
                masked = ph == 1 and i >= SEL0
                if masked:
                    pe.wait_ge(mask_made, TILES - SEL0)
                for c in range(0, length, HALF):
                    w = min(HALF, length - c)
                    o = score_of(u, c, c + w)
                    pe.matmul(o, q[:, qt], k[:, c:c + w], start=True, stop=False)
                    near = max(c, length - BAND)
                    banded = masked and near < c + w
                    ins = pe.matmul(o, q[rows, qt], kT_r[rows, b, c:c + w], start=False, stop=not banded)
                    if banded:
                        mk = mask[:, score_off[i] + near:score_off[i] + c + w]
                        ins = pe.matmul(score_of(u, near, c + w), identb[:, :], mk, start=False, stop=True)
                ins.then_inc(s_ready, 1)

            def turn(ph, s, quad):
                q, m, j, nj = quad
                if ph == 0:
                    pe.wait_ge(combined, s + 1)
                else:
                    pe.wait_ge(exp_done, (STEPS + s) * 2 + m + 1)
                if q >= 2:
                    wait_moved(q - 2)
                p = probs_of(ph, s, m)
                for k in range(nj):
                    ins = pe.transpose(bank(T_BANK + q % 2)[:, k * P:(k + 1) * P],
                                       p[:, (j + k) * P:(j + k + 1) * P], ident[:, :])
                ins.then_inc(t_ready, 1)

            def weigh(ph, s, quad):
                q, m, j, nj = quad
                b, i = place_of(ph, s)
                n = ph * STEPS + s
                if j == 0 and m == 0 and n >= 1:
                    pe.wait_ge(o_moved, n)
                wait_moved(q)
                if ph == 0:
                    cols, o = slice(b * P, (b + 1) * P), bank(O_BANK)[:, 0:P]
                else:
                    cols = slice(b * P + m * HEAD, b * P + (m + 1) * HEAD)
                    o = bank(O_BANK)[:, m * HEAD:(m + 1) * HEAD]
                for k in range(nj):
                    ins = pe.matmul(o, probsT[ph][:, q % 4, k * P:(k + 1) * P], v[:, j + k, cols],
                                    start=(j + k == 0), stop=(j + k == i))
                ins.then_inc(pv_done, 1)

            def attend(ph):
                lag = 1 if ph == 0 else 0
                scores(ph, 0, 0)
                scores(ph, 0, 1)
                for s in range(STEPS + lag):
                    t = s - lag
                    qs = quads[ph, t] if t >= 0 else []
                    if s + 1 < STEPS:
                        scores(ph, s + 1, 0)
                    if t == 0:
                        pe.wait_ge(bank_moved, moved[(A_GROUPS, B_GROUPS)[ph][-1] + 1])
                    for quad in qs[0:2]:
                        turn(ph, t, quad)
                    if s + 1 < STEPS:
                        scores(ph, s + 1, 1)
                    for k, quad in enumerate(qs):
                        if 2 <= k + 1 < len(qs):
                            turn(ph, t, qs[k + 1])
                        weigh(ph, t, quad)

            attend(0)
            for g in B_GROUPS:
                project(g)
            attend(1)

            def turn_mix(t):
                for half in range(2):
                    n = 2 * t + half
                    if t >= 2:
                        pe.wait_ge(mixT_lo, n - 3)
                    src = mixA if half == 0 else mixB
                    for c in range(4):
                        ins = pe.transpose(bank(n % 4)[:, c * P:(c + 1) * P], src[:, t, c * P:(c + 1) * P],
                                           ident[:, :])
                    ins.then_inc(mixT_ready, 1)

            pe.wait_ge(mixA_done, STEPS)
            pe.wait_ge(o_moved, 2 * STEPS)
            turn_mix(0)
            for t in range(TILES):
                if t + 1 < TILES:
                    turn_mix(t + 1)
                pe.wait_ge(mixT_lo, 2 * t + 2)
                for half in range(2):
                    if t >= 2:
                        pe.wait_ge(y_summed, 2 * (t - 2) + half + 1)
                    cols = slice(half * HALF, (half + 1) * HALF)
                    o = bank(4 + 2 * (t % 2) + half)
                    for e in range(DB):
                        if t == 0:
                            pe.wait_ge(w_lo_made, CHUNKS + 2 * e + half + 1)
                        for k, (a, w) in enumerate(((mx_hi, big_hi), (mx_hi, big_lo), (mx_lo, big_hi))):
                            ins = pe.matmul(o, a[:, t % 2, e, :], w[:, e, cols],
                                            start=(e == 0 and k == 0), stop=(e == DB - 1 and k == 2))
                    ins.then_inc(y_ready, 1)

        @block.vector
        def _(dve):
            own = [0]

            def link(ins):
                own[0] += 1
                ins.then_inc(dve_own, 1)
                dve.wait_ge(dve_own, own[0])

            def inverse_root(root, var, done, a):
                link(dve.reciprocal(root, root))
                link(dve.tensor_tensor(a, root, root, ALU.mult))
                link(dve.tensor_tensor(a, a, var, ALU.mult))
                link(dve.tensor_scalar(a, a, -0.5, 1.5, ALU.mult, ALU.add))
                ins = dve.tensor_tensor(root, root, a, ALU.mult)
                if done is None:
                    link(ins)
                else:
                    ins.then_inc(done, 1)

            nh = A_HEADS + B_HEADS

            def low_h(n):
                half, d = divmod(n, DB)
                cols = slice(half * HALF, (half + 1) * HALF)
                dve.wait_ge(hT_hi, n + 1)
                dve.scalar_tensor_tensor(out=big_lo[:, d, cols], in0=bank(d), scalar=nw[:, d:d + 1],
                                         in1=big_hi[:, d, cols].bitcast(f32), op0=ALU.mult,
                                         op1=ALU.subtract).then_inc(hT_lo, 1)

            dve.memset(warm, 1.0).then_inc(warm_made, 1)
            dve.wait_ge(nw_turned, 1)
            dve.tensor_copy(nw[:, :], bank(7)[:, 0:DB]).then_inc(nw_moved, 1)
            for t in range(0, TILES, 2):
                two = slice(t, t + 2)
                dve.wait_ge(x_squared, t + 2)
                dve.tensor_scalar(varx[:, two], ssx[:, two], 1.0 / D_MODEL, EPS, ALU.mult, ALU.add
                                  ).then_inc(x_var, 1)
                if t == TILES - 2:
                    low_h(0)
                dve.wait_ge(x_root, t // 2 + 1)
                inverse_root(rstd[:, two], varx[:, two], x_rstd, t_a)
                dve.wait_ge(x_rstd, t // 2 + 1)
                dve.tensor_scalar(xs[:, t, :], xs[:, t, :], rstd[:, t:t + 1], None, ALU.mult
                                  ).then_inc(x_scaled[0], 1)
            for n in range(1, 2 * DB):
                low_h(n)
            dve.wait_ge(consts_loaded, 16 * 5)
            for m in range(2):
                link(dve.tensor_tensor(lam4[:, 2 * m, :], lam4[:, 2 * m, :], lam4[:, 2 * m + 1, :], ALU.mult))
            for m in range(2):
                dve.reduce_sum(lam_s[:, m:m + 1], lam4[:, 2 * m, :], AX.X).then_inc(lam_sums, 1)
            for h in range(nh):
                dve.wait_ge(band_ready, h + 1)
                dve.tensor_copy(band[:, h, :], bank(6 + h % 2)[:, 0:RELS]).then_inc(band_out, 1)
            dve.wait_ge(bank_ready, 2)
            dve.tensor_copy(ikT[0:HEAD, HALF:SEQ], bank(1)[0:HEAD, :])
            dve.tensor_copy(ikT[HEAD:P, HALF:SEQ], bank(1)[0:HEAD, :])
            dve.tensor_scalar(iwT[:, HALF:SEQ], bank(1)[HEAD:HEAD + IDX_HEADS, :], IDX_SCALE, None, ALU.mult
                              ).then_inc(ik_moved, 1)
            dve.wait_ge(iw_ready, 1)
            dve.tensor_copy(iw[:, :], bank(7)[:, 0:TILES * IDX_HEADS]).then_inc(iw_moved, 1)
            dve.wait_ge(iw_moved, 1)
            n = 0
            for i in range(SEL0, TILES):
                sc = score[:, score_off[i]:score_off[i] + P * (i + 1)]
                for h in range(IDX_HEADS):
                    dve.wait_ge(idx_relu, n + 1)
                    r = relu[:, n % 2, 0:P * (i + 1)]
                    wcol = iw[:, i * IDX_HEADS + h:i * IDX_HEADS + h + 1]
                    if h == 0:
                        ins = dve.tensor_scalar(sc, r, wcol, None, ALU.mult)
                    else:
                        dve.wait_ge(idx_added, n)
                        ins = dve.scalar_tensor_tensor(out=sc, in0=r, scalar=wcol, in1=sc, op0=ALU.mult,
                                                       op1=ALU.add)
                    ins.then_inc(idx_added, 1)
                    n += 1
                dve.wait_ge(idx_added, n)
                link(dve.memset(score[0:CHUNK, score_off[i] + P * (i + 1) - CHUNK:
                                      score_off[i] + P * (i + 1)], UNSEEN))

            dve.wait_ge(lam_exp, 1)
            link(dve.tensor_tensor(neglam, lam_e[:, 1:2], lam_e[:, 0:1], ALU.subtract))
            link(dve.tensor_scalar(neglam, neglam, -LAMBDA_INIT, None, ALU.add))
            dve.wait_ge(bias_loaded, 16 * A_HEADS)
            link(dve.memset(bias[0:CHUNK, 0:A_HEADS, BAND - CHUNK:BAND], MASKED))

            def select(rounds, first=SEL0, end=TILES):
                for _ in range(rounds):
                    for i in range(first, end):
                        sc = score[:, score_off[i]:score_off[i] + P * (i + 1)]
                        ins = dve.max(top8[:, i - SEL0, :], sc)
                        if i == end - 1:
                            link(ins)
                    for i in range(first, end):
                        sc = score[:, score_off[i]:score_off[i] + P * (i + 1)]
                        ins = dve.match_replace(sc, top8[:, i - SEL0, :], sc, TAKEN)
                        if i == end - 1:
                            link(ins)

            def later(ins):
                own[0] += 1
                ins.then_inc(dve_own, 1)
                return own[0]

            far_done, inverted, factor_done = {}, {}, {}

            def far_min(ph, s, m):
                i = place_of(ph, s)[1]
                far = P * (i + 1) - min(BAND, P * (i + 1))
                u = (ph * STEPS + s) * 2 + m
                dve.wait_ge(s_ready, u + 1)
                if far:
                    least = farmin[:, u % 4:u % 4 + 1]
                    o = score_of(u, 0, far)
                    if ph == 0:
                        ins = dve.tensor_reduce(least, o, AX.X, ALU.min)
                    else:
                        ins = dve.tensor_tensor_reduce(
                            out=o, in0=o, in1=mask[:, score_off[i]:score_off[i] + far], scale=1.0,
                            scalar=UNSEEN_MIN, op0=ALU.add, op1=ALU.min, accum_out=least)
                    far_done[u] = later(ins)

            def soften(ph, s, m):
                b, i = place_of(ph, s)
                length = P * (i + 1)
                w = min(BAND, length)
                u = (ph * STEPS + s) * 2 + m
                h = b if ph == 0 else A_HEADS + 2 * b + m
                least = UNSEEN_MIN
                if u in far_done:
                    dve.wait_ge(dve_own, far_done[u])
                    least = farmin[:, u % 4:u % 4 + 1]
                o = score_of(u, length - w, length)
                dve.tensor_tensor_reduce(out=o, in0=o, in1=bias[:, h, BAND - w:BAND], scale=1.0,
                                         scalar=least, op0=ALU.add, op1=ALU.min,
                                         accum_out=negmax[:, u % 4:u % 4 + 1]).then_inc(max_ready, 1)

            def invert(ph, s):
                c = 2 * s % 8
                dve.wait_ge(exp_done, 2 * (ph * STEPS + s) + 2)
                inverted[ph, s] = later(dve.reciprocal(rinv[:, c:c + 2], rsum[:, c:c + 2]))

            def turned(ph, quads):
                for q, m, j, nj in quads:
                    if mover[q] == 1:
                        dve.wait_ge(t_ready, q + 1)
                        if q >= 4:
                            dve.wait_ge(pv_done, q - 3)
                        dve.tensor_copy(probsT[ph][:, q % 4, 0:nj * P], bank(T_BANK + q % 2)[:, 0:nj * P]
                                        ).then_inc(t_moved[1], 1)

            def factor(s):
                c = 2 * s % 8
                dve.wait_ge(dve_own, inverted[0, s])
                factor_done[s] = later(dve.scalar_tensor_tensor(
                    out=comb_c[:, s % 2:s % 2 + 1], in0=rsum[:, c:c + 1], scalar=neglam,
                    in1=rinv[:, c + 1:c + 2], op0=ALU.mult, op1=ALU.mult))

            def combine(s):
                dve.wait_ge(dve_own, factor_done[s])
                length = P * (place_of(0, s)[1] + 1)
                p1, p2 = (probs_of(0, s, m)[:, 0:length] for m in range(2))
                dve.scalar_tensor_tensor(out=p1, in0=p2, scalar=comb_c[:, s % 2:s % 2 + 1], in1=p1,
                                         op0=ALU.mult, op1=ALU.add).then_inc(combined, 1)

            def finishA(s):
                dve.wait_ge(pv_done, quads_through(0, s))
                if s >= 4:
                    dve.wait_ge(o_gated, s - 3)
                    dve.wait_ge(o_squared, s - 3)
                dve.tensor_scalar(o_tmp[:, s % 4, :], bank(O_BANK)[:, 0:P],
                                  rinv[:, 2 * s % 8:2 * s % 8 + 1], None, ALU.mult).then_inc(o_moved, 1)

            ROUNDS = TOPK // 8
            FIRST = ROUNDS // 2
            select(FIRST)
            select(1, TILES - 2)
            far_min(0, 0, 0)
            soften(0, 0, 0)
            far_min(0, 0, 1)
            soften(0, 0, 1)
            for s in range(STEPS):
                if s >= 2:
                    finishA(s - 2)
                if s + 1 < STEPS:
                    far_min(0, s + 1, 0)
                invert(0, s)
                if s + 1 < STEPS:
                    soften(0, s + 1, 0)
                factor(s)
                combine(s)
                if s + 1 < STEPS:
                    far_min(0, s + 1, 1)
                    soften(0, s + 1, 1)
            finishA(STEPS - 2)
            finishA(STEPS - 1)
            dve.wait_ge(o_squared, STEPS)
            link(dve.tensor_scalar(ssA, ssA, 1.0 / P, EPS, ALU.mult, ALU.add))
            dve.tensor_copy(t_a[:, 0:1], ssA[:, 0:1]).then_inc(varA, 1)
            dve.wait_ge(rootA, 1)
            inverse_root(rA, ssA, rstdA, iw[:, 0:STEPS])
            dve.wait_ge(bias_loaded, 16 * nh)
            link(dve.memset(bias[0:CHUNK, A_HEADS:nh, BAND - CHUNK:BAND], MASKED))
            select(ROUNDS - FIRST - 1)
            select(1, SEL0, TILES - 2)
            for i in range(SEL0, TILES):
                o = slice(score_off[i], score_off[i] + P * (i + 1))
                dve.tensor_scalar(mask[:, o], score[:, o], TAKEN, MASKED, ALU.not_equal, ALU.mult
                                  ).then_inc(mask_made, 1)

            def finishB(s):
                b, i = place_of(1, s)
                c = 2 * s % 8
                dve.wait_ge(dve_own, inverted[1, s])
                dve.wait_ge(pv_done, quads_through(1, s))
                for m in range(2):
                    g = mixB[:, i, b * P + m * HEAD:b * P + (m + 1) * HEAD]
                    ins = dve.scalar_tensor_tensor(out=g, in0=bank(O_BANK)[:, m * HEAD:(m + 1) * HEAD],
                                                   scalar=rinv[:, c + m:c + m + 1], in1=g, op0=ALU.mult,
                                                   op1=ALU.mult)
                ins.then_inc(o_moved, 1)

            far_min(1, 0, 0)
            soften(1, 0, 0)
            far_min(1, 0, 1)
            soften(1, 0, 1)
            dve.wait_ge(bank_moved, moved[9])
            for s in range(STEPS + 1):
                qs = quads[1, s] if s < STEPS else []
                if s >= 1:
                    invert(1, s - 1)
                    finishB(s - 1)
                if s + 1 < STEPS:
                    far_min(1, s + 1, 0)
                turned(1, qs[0:1])
                if s + 1 < STEPS:
                    soften(1, s + 1, 0)
                turned(1, qs[1:2])
                if s + 1 < STEPS:
                    far_min(1, s + 1, 1)
                    soften(1, s + 1, 1)
                turned(1, qs[2:])

            for t in range(TILES + 1):
                if t < TILES:
                    for half in range(2):
                        n = 2 * t + half
                        dve.wait_ge(mixT_hi, n + 1)
                        blk = slice(half * 4, half * 4 + 4)
                        dve.tensor_tensor(mx_lo[:, t % 2, blk, :],
                                          bank(n % 4)[:, :].rearrange("p (c q) -> p c q", q=P),
                                          mx_hi[:, t % 2, blk, :].bitcast(f32), ALU.subtract
                                          ).then_inc(mixT_lo, 1)
                if t >= 1:
                    k = t - 1
                    dve.wait_ge(xres_loaded[k % 2], 16 * (k // 2 + 1))
                    if k >= 2:
                        dve.wait_ge(y_squared, 2 * k - 2)
                        dve.wait_ge(y_scaled, 2 * k - 2)
                    for half in range(2):
                        cols = slice(half * HALF, (half + 1) * HALF)
                        dve.wait_ge(y_ready, 2 * k + half + 1)
                        dve.tensor_tensor(y[:, k % 2, cols], bank(4 + 2 * (k % 2) + half),
                                          xres[:, k % 2, cols], ALU.add).then_inc(y_summed, 1)
                    dve.wait_ge(y_squared, 2 * k + 2)
                    link(dve.tensor_tensor(t_a[:, 0:1], ssA[:, 2 * k:2 * k + 1], ssA[:, 2 * k + 1:2 * k + 2],
                                           ALU.add))
                    dve.tensor_scalar(varx[:, k:k + 1], t_a[:, 0:1], 1.0 / D_MODEL, EPS, ALU.mult, ALU.add
                                      ).then_inc(y_var, 1)
                    dve.wait_ge(y_root, k + 1)
                    inverse_root(rstd[:, k:k + 1], varx[:, k:k + 1], None, t_a[:, 0:1])
                    dve.wait_ge(fw_loaded, 16)
                    if k >= 2:
                        dve.wait_ge(stored[k % 2], 32 * (k // 2))
                    for half in range(2):
                        cols = slice(half * HALF, (half + 1) * HALF)
                        dve.scalar_tensor_tensor(out=y_out[:, k % 2, cols], in0=y[:, k % 2, cols],
                                                 scalar=rstd[:, k:k + 1], in1=fw[:, cols], op0=ALU.mult,
                                                 op1=ALU.mult).then_inc(y_scaled, 1)


INPUTS = ["x", "norm_w", "w_in", "w_out", "lambda_q1", "lambda_k1", "lambda_q2", "lambda_k2",
          "subln_w", "rel_bias", "final_norm_w"]


def kernel(**inputs):
    import concourse.bacc as bacc
    from concourse.bass_utils import run_bass_kernel_spmd

    nc = bacc.Bacc("TRN2", target_bir_lowering=False, num_devices=1)
    f32 = mybir.dt.float32
    arrays, args = {}, []
    for name in INPUTS:
        arrays[f"in_{name}"] = np.ascontiguousarray(inputs[name])
    arrays["in_selector"] = bucket_selector()
    for name, a in arrays.items():
        args.append(nc.dram_tensor(name, a.shape, f32, kind="ExternalInput").ap())
    args.append(nc.dram_tensor("out_y", (1, SEQ, D_MODEL), f32, kind="ExternalOutput").ap())
    build(nc, *args)
    r = run_bass_kernel_spmd(nc, [arrays], core_ids=[0])
    return r.results[0]["out_y"]
```
